# Optimizing a Trainium2 kernel written in Bass

```python
import jax, jax.numpy as jnp
from jax import lax
import numpy as np

D_MODEL = 1024
BATCH = 1
SEQ = 256
DEPTH = 2

N_MIXERS = 2
N_A_LAYERS = (DEPTH + 1) // 2
N_B_LAYERS = DEPTH // 2

N_HEADS = 16
HEAD_DIM = 64
N_KV_HEADS = 4
GROUP = N_HEADS // N_KV_HEADS
IDX_HEADS = 8
IDX_DIM = 64
TOPK_MAX = 256
Q_BLOCK = 128
Q_W = N_HEADS * HEAD_DIM
KV_W = N_KV_HEADS * HEAD_DIM
IQ_W = IDX_HEADS * IDX_DIM
DSA_WIDTHS = (Q_W, KV_W, KV_W, IQ_W, IDX_DIM, IDX_HEADS)
DSA_IN = sum(DSA_WIDTHS)
DSA_SPLITS = tuple(int(s) for s in np.cumsum(DSA_WIDTHS)[:-1])

RWKV_HEAD = 64
RWKV_HEADS = D_MODEL // RWKV_HEAD
DECAY_LORA = 64
AAA_LORA = 64
GATE_LORA = 160
GN_EPS = 64e-5

D_FF = 2816
N_MOD = 9
RMS_EPS = 1e-6

kernel_name = "hybrid_dsa_rwkv7_macaron_adaln"

def rms(x):
    xf = x.astype(jnp.float32)
    return (xf * lax.rsqrt(jnp.mean(xf * xf, axis=-1, keepdims=True) + RMS_EPS)).astype(x.dtype)

def modulate(h, shift, scale):
    return rms(h) * (1 + scale[:, None, :]) + shift[:, None, :]

def swiglu(x, w_gu, w_down):
    gate, up = jnp.split(x @ w_gu, 2, axis=-1)
    return (jax.nn.silu(gate) * up) @ w_down

def dsa_mixer(x, w_in, q_norm, k_norm, ik_norm, w_out):
    B, S, _ = x.shape
    k_top = min(TOPK_MAX, S // 4)
    q, k, v, iq, ik, iw = jnp.split(x @ w_in, DSA_SPLITS, axis=-1)
    q = rms(q.reshape(B, S, N_KV_HEADS, GROUP, HEAD_DIM)) * q_norm
    k = rms(k.reshape(B, S, N_KV_HEADS, HEAD_DIM)) * k_norm
    v = v.reshape(B, S, N_KV_HEADS, HEAD_DIM)
    iq = iq.reshape(B, S, IDX_HEADS, IDX_DIM)
    ik = rms(ik) * ik_norm
    iw = iw * (IDX_HEADS ** -0.5 * IDX_DIM ** -0.5)
    nb = S // Q_BLOCK
    key_pos = jnp.arange(S)

    def to_blocks(a):
        return jnp.moveaxis(a.reshape(B, nb, Q_BLOCK, *a.shape[2:]), 1, 0)

    def block(args):
        qb, iqb, iwb, start = args
        qpos = start + jnp.arange(Q_BLOCK)
        rel = jax.nn.relu(jnp.einsum('bqhd,bsd->bqhs', iqb, ik))
        score = jnp.einsum('bqhs,bqh->bqs', rel, iwb).astype(jnp.float32)
        causal = key_pos[None, :] <= qpos[:, None]
        score = jnp.where(causal[None], score, -jnp.inf)
        _, sel = lax.top_k(score, k_top)
        valid = sel <= qpos[None, :, None]
        k_sel = jax.vmap(lambda kk, ii: kk[ii])(k, sel)
        v_sel = jax.vmap(lambda vv, ii: vv[ii])(v, sel)
        logits = jnp.einsum('bqhgd,bqkhd->bqhgk', qb, k_sel).astype(jnp.float32) * (HEAD_DIM ** -0.5)
        logits = jnp.where(valid[:, :, None, None, :], logits, -jnp.inf)
        p = jax.nn.softmax(logits, axis=-1).astype(v.dtype)
        return jnp.einsum('bqhgk,bqkhd->bqhgd', p, v_sel)

    starts = jnp.arange(nb, dtype=jnp.int32) * Q_BLOCK
    o = lax.map(block, (to_blocks(q), to_blocks(iq), to_blocks(iw), starts))
    o = jnp.moveaxis(o, 0, 1).reshape(B, S, Q_W)
    return o @ w_out

def rwkv7_mixer(x, mu, w_rkv, w0, w1, w2, a0, a1, a2, g1, g2, k_k, k_a, r_k, ln_w, ln_b, w_out):
    B, S, D = x.shape
    H, N = RWKV_HEADS, RWKV_HEAD
    f32 = jnp.float32
    xx = jnp.pad(x, ((0, 0), (1, 0), (0, 0)))[:, :-1] - x
    xrkv = x[None] + xx[None] * mu[:3, None, None, :]
    r, k, v = jnp.einsum('nbsd,nde->nbse', xrkv, w_rkv)
    xw = x + xx * mu[3]
    xa = x + xx * mu[4]
    xg = x + xx * mu[5]
    w_log = -jax.nn.softplus(-(w0 + jnp.tanh(xw @ w1) @ w2)) - 0.5
    decay = jnp.exp(-jnp.exp(w_log.astype(f32)))
    a = jax.nn.sigmoid(a0 + (xa @ a1) @ a2)
    g = jax.nn.sigmoid(xg @ g1) @ g2
    kk = (k * k_k).astype(f32).reshape(B, S, H, N)
    kk = kk / jnp.maximum(jnp.sqrt(jnp.sum(kk * kk, axis=-1, keepdims=True)), 1e-12)
    k = k * (1 + (a - 1) * k_a)
    rh = r.astype(f32).reshape(B, S, H, N)
    kh = k.astype(f32).reshape(B, S, H, N)
    vh = v.astype(f32).reshape(B, S, H, N)
    ah = a.astype(f32).reshape(B, S, H, N)
    wh = decay.reshape(B, S, H, N)
    bh = kk * ah

    def step(state, inp):
        r_t, w_t, k_t, v_t, kk_t, b_t = inp
        sa = jnp.einsum('bhvk,bhk->bhv', state, -kk_t)
        state = (state * w_t[:, :, None, :] + sa[..., None] * b_t[:, :, None, :]
                 + v_t[..., None] * k_t[:, :, None, :])
        return state, jnp.einsum('bhvk,bhk->bhv', state, r_t)

    tf = lambda t: jnp.moveaxis(t, 1, 0)
    state0 = jnp.zeros((B, H, N, N), f32)
    _, y = lax.scan(step, state0, (tf(rh), tf(wh), tf(kh), tf(vh), tf(kk), tf(bh)))
    y = jnp.moveaxis(y, 0, 1)
    mean = jnp.mean(y, axis=-1, keepdims=True)
    var = jnp.mean(jnp.square(y - mean), axis=-1, keepdims=True)
    yn = ((y - mean) * lax.rsqrt(var + GN_EPS)).reshape(B, S, D) * ln_w.astype(f32) + ln_b.astype(f32)
    bonus = (jnp.sum(rh * kh * r_k.astype(f32), axis=-1, keepdims=True) * vh).reshape(B, S, D)
    out = ((yn + bonus).astype(x.dtype)) * g
    return out @ w_out

def setup_inputs(seed: int = 0) -> dict:
    key = jax.random.key(seed)
    ks = jax.random.split(key, 32)
    f32 = jnp.float32
    D = D_MODEL

    def nrm(k, shape, fan_in, scale=1.0):
        return jax.random.normal(k, shape, f32) * (scale * fan_in ** -0.5)

    def near_one(k, shape):
        return 1.0 + 0.02 * jax.random.normal(k, shape, f32)

    return {
        "x": jax.random.normal(ks[0], (BATCH, SEQ, D), f32),
        "c": jax.random.normal(ks[1], (BATCH, D), f32),
        "ada_w": nrm(ks[2], (DEPTH, D, N_MOD * D), D, 0.5),
        "ada_b": 0.02 * jax.random.normal(ks[3], (DEPTH, N_MOD * D), f32),
        "ffn_w_gu": nrm(ks[4], (DEPTH, 2, D, 2 * D_FF), D),
        "ffn_w_down": nrm(ks[5], (DEPTH, 2, D_FF, D), D_FF),
        "dsa_w_in": nrm(ks[6], (N_A_LAYERS, D, DSA_IN), D),
        "dsa_q_norm": near_one(ks[7], (N_A_LAYERS, HEAD_DIM)),
        "dsa_k_norm": near_one(ks[8], (N_A_LAYERS, HEAD_DIM)),
        "dsa_ik_norm": near_one(ks[9], (N_A_LAYERS, IDX_DIM)),
        "dsa_w_out": nrm(ks[10], (N_A_LAYERS, Q_W, D), Q_W),
        "rwkv_mu": jax.random.uniform(ks[11], (N_B_LAYERS, 6, D), f32),
        "rwkv_w_rkv": nrm(ks[12], (N_B_LAYERS, 3, D, D), D),
        "rwkv_w0": jax.random.uniform(ks[13], (N_B_LAYERS, D), f32, -6.0, -1.0),
        "rwkv_w1": nrm(ks[14], (N_B_LAYERS, D, DECAY_LORA), D),
        "rwkv_w2": nrm(ks[15], (N_B_LAYERS, DECAY_LORA, D), DECAY_LORA, 0.1),
        "rwkv_a0": 0.1 * jax.random.normal(ks[16], (N_B_LAYERS, D), f32),
        "rwkv_a1": nrm(ks[17], (N_B_LAYERS, D, AAA_LORA), D),
        "rwkv_a2": nrm(ks[18], (N_B_LAYERS, AAA_LORA, D), AAA_LORA, 0.5),
        "rwkv_g1": nrm(ks[19], (N_B_LAYERS, D, GATE_LORA), D),
        "rwkv_g2": nrm(ks[20], (N_B_LAYERS, GATE_LORA, D), GATE_LORA),
        "rwkv_k_k": 0.85 + 0.02 * jax.random.normal(ks[21], (N_B_LAYERS, D), f32),
        "rwkv_k_a": near_one(ks[22], (N_B_LAYERS, D)),
        "rwkv_r_k": 0.1 * jax.random.normal(ks[23], (N_B_LAYERS, RWKV_HEADS, RWKV_HEAD), f32),
        "rwkv_ln_w": near_one(ks[24], (N_B_LAYERS, D)),
        "rwkv_ln_b": 0.02 * jax.random.normal(ks[25], (N_B_LAYERS, D), f32),
        "rwkv_w_out": nrm(ks[26], (N_B_LAYERS, D, D), D),
    }

def reference(x, c, ada_w, ada_b, ffn_w_gu, ffn_w_down, dsa_w_in, dsa_q_norm, dsa_k_norm,
              dsa_ik_norm, dsa_w_out, rwkv_mu, rwkv_w_rkv, rwkv_w0, rwkv_w1, rwkv_w2, rwkv_a0,
              rwkv_a1, rwkv_a2, rwkv_g1, rwkv_g2, rwkv_k_k, rwkv_k_a, rwkv_r_k, rwkv_ln_w,
              rwkv_ln_b, rwkv_w_out):
    h = x
    c_act = jax.nn.silu(c)
    for i in range(DEPTH):
        mod = c_act @ ada_w[i] + ada_b[i]
        sh1, sc1, gt1, sh2, sc2, gt2, sh3, sc3, gt3 = jnp.split(mod, N_MOD, axis=-1)
        h = h + 0.5 * gt1[:, None, :] * swiglu(modulate(h, sh1, sc1), ffn_w_gu[i, 0], ffn_w_down[i, 0])
        u = modulate(h, sh2, sc2)
        j = i // N_MIXERS
        if i % N_MIXERS == 0:
            m = dsa_mixer(u, dsa_w_in[j], dsa_q_norm[j], dsa_k_norm[j], dsa_ik_norm[j], dsa_w_out[j])
        else:
            m = rwkv7_mixer(u, rwkv_mu[j], rwkv_w_rkv[j], rwkv_w0[j], rwkv_w1[j], rwkv_w2[j],
                            rwkv_a0[j], rwkv_a1[j], rwkv_a2[j], rwkv_g1[j], rwkv_g2[j],
                            rwkv_k_k[j], rwkv_k_a[j], rwkv_r_k[j], rwkv_ln_w[j], rwkv_ln_b[j],
                            rwkv_w_out[j])
        h = h + gt2[:, None, :] * m
        h = h + 0.5 * gt3[:, None, :] * swiglu(modulate(h, sh3, sc3), ffn_w_gu[i, 1], ffn_w_down[i, 1])
    return h


_drawn_inputs = setup_inputs


def setup_inputs(seed=0):
    import zlib

    import numpy as np

    out = dict(_drawn_inputs(seed))
    spreads = {}
    factors = {'dsa_q_norm': 8.0,
     'dsa_k_norm': 8.0,
     'dsa_ik_norm': 8.0,
     'rwkv_w1': 8.0,
     'rwkv_w2': 8.0,
     'rwkv_a0': 7.772,
     'rwkv_k_k': 8.0,
     'rwkv_k_a': 8.0,
     'rwkv_ln_w': 8.0,
     'rwkv_ln_b': 8.0}
    for name, (base, spread) in spreads.items():
        noise = np.random.default_rng([zlib.crc32(name.encode()), seed]).standard_normal(out[name].shape)
        drawn = base * np.exp(spread * noise) if base else spread * noise
        out[name] = __import__('jax').numpy.asarray(drawn.astype(out[name].dtype))
    for name, factor in factors.items():
        out[name] = (out[name] * factor).astype(out[name].dtype)
    return out
```

```python
from contextlib import ExitStack

import concourse.bass as bass
from concourse import mybir

P = 128
F32 = mybir.dt.float32
F32R = mybir.dt.float32r
BF16 = mybir.dt.bfloat16
ALU = mybir.AluOpType
ACT = mybir.ActivationFunctionType
AX = mybir.AxisListType

RMS_EPS = 1e-6


def trunk(nc, a, out):
    SEQ, D = a["x"].shape[1:]
    TT = SEQ // P
    KD = D // P
    FF = a["ffn_w_down"].shape[2]
    FB = 256
    NB = FF // FB
    HD = 64
    QH = a["dsa_w_out"].shape[1] // HD
    KVH = 4
    IH = 8
    TOPK = min(256, SEQ // 4)
    DSA_SMALL = HD + IH
    CH = 32
    NC = SEQ // CH
    RH = a["rwkv_r_k"].shape[1]
    WA, GL = a["rwkv_w1"].shape[2], a["rwkv_g1"].shape[2]
    DECAY = 0.6065306597126334
    GN_EPS = 64e-5
    NEG = -3.0e38
    TAKEN = -3.4e38
    HIDDEN = -1.0e30
    HALF = 512
    NMOD = a["ada_w"].shape[2] // D
    HV = NMOD * D // HALF
    assert TT == 2 and KD == 8 and FF == NB * FB and NB == 11

    FFN_BLOCK0 = (0, 18, 29, 48)
    ADA_FRONT = 4
    ADA_FFN = ((4, NB), (18, NB), (29, 7), (36, 0))

    ctx = ExitStack()
    with ctx:
        ctx.enter_context(nc.allow_non_contiguous_dma(reason="columns of small vectors"))

        def sb(name, shape, dt=F32):
            return ctx.enter_context(nc.sbuf_tensor(name, shape, dt))

        def sem(name):
            return ctx.enter_context(nc.semaphore(name))

        top = {"at": -(-nc.sbuf_base // 64) * 64}

        def place(name, shape, dt=F32, at=None):
            size = 1
            for n in shape[1:]:
                size *= n
            size *= 2 if dt == BF16 else 4
            start = top["at"] if at is None else at
            t = nc.alloc_sbuf_tensor_at(name, shape, dt, offset=start)
            if at is None:
                top["at"] = -(-(start + size) // 32) * 32
            return t

        gu_hi_at = top["at"]
        gu_hi = place("gu_hi", [P, 2, KD, HALF], F32R)
        gu_lo = place("gu_lo", [P, 2, KD, HALF], F32R)
        raw = place("raw", [P, 3, 4 * HALF])
        mods_at = top["at"]
        mods = place("mods", [P, HV, HALF])
        h = place("h", [P, TT, D])
        xT_at = top["at"]
        xT_hi = place("xT_hi", [P, KD, SEQ], F32R)
        xT_lo = place("xT_lo", [P, KD, SEQ], F32R)
        ident = place("ident", [P, P])
        ones = place("ones", [P, P])
        ccol = place("ccol", [P, KD])
        cact = place("cact", [P, KD])
        stat = place("stat", [P, 16])
        masks = place("masks", [P, 2, P])
        block_ones = place("block_ones", [P, P])
        mu = place("mu", [P, 6, KD])
        cols = place("cols", [P, 5, KD])
        rk_heads = place("rk_heads", [P, KD, 2])
        chunk_decay = place("chunk_decay", [P, KD, NC])
        rstat = place("rstat", [P, 96])
        head_gain = place("head_gain", [P, 3])
        dn_at = top["at"]
        dn_hi = place("dn_hi", [P, 2, D], F32R)
        dn_lo = place("dn_lo", [P, 2, D], F32R)
        hT_at = top["at"]
        hT_hi = place("hT_hi", [P, TT, 2, P], F32R)
        hT_lo = place("hT_lo", [P, TT, 2, P], F32R)
        hid_at = top["at"]
        hid = place("hid", [P, TT, FB])
        xn_at = top["at"]
        xn = place("xn", [P, 2, HALF])
        junk_at = top["at"]
        junk = place("junk", [P, D], BF16)
        ada_at = top["at"]
        ada_raw = place("ada_raw", [P, 4, 2, HALF])
        ada_acc = place("ada_acc", [P, HALF])
        ada_bias = place("ada_bias", [P, HALF])
        spare_at = top["at"]

        z = place("z", [P, TT, 4 * HALF], at=dn_at)
        qT = place("qT", [P, QH // 2, SEQ], at=xT_at)
        kT = place("kT", [P, KVH, SEQ], at=xT_at + 8192)
        iqT = place("iqT", [P, IH // 2, SEQ], at=xT_at + 12288)
        score = place("score", [P, TT, SEQ], at=hT_at)
        offset = place("offset", [P, TT, SEQ], at=hT_at + 2048)
        relu = place("relu", [P, 2, HALF], at=xn_at)
        squares = place("squares", [P, D], at=xn_at)
        r0 = mods_at
        v_tok = place("v_tok", [P, TT, D], at=r0)
        g_tok = place("g_tok", [P, TT, D], at=r0 + 8192)
        hid_wa = place("hid_wa", [P, SEQ], at=r0 + 16384)
        hid_g = place("hid_g", [P, 2, SEQ], at=r0 + 16384 + 1024)
        K1 = 1024
        uT = place("uT", [P, KD, SEQ], at=dn_at)
        xxT = place("xxT", [P, KD, SEQ], at=dn_at + 8 * K1)
        rT = place("rT", [P, KD, SEQ], at=dn_at + 16 * K1)
        kTc = place("kTc", [P, KD, SEQ], at=dn_at + 24 * K1)
        sigT = place("sigT", [P, KD, SEQ], at=dn_at + 32 * K1)
        aT = place("aT", [P, KD, SEQ], at=dn_at + 40 * K1)
        mix = [place("mix_w", [P, KD, SEQ], at=xT_at), place("mix_a", [P, KD, SEQ], at=xT_at + 8192),
               place("mix_tmp", [P, KD, SEQ], at=dn_at + 48 * K1)]
        wa2 = place("wa2", [P, D], at=dn_at + 16 * K1)
        g2 = place("g2", [P, 2, D], at=dn_at + 20 * K1)
        w1 = place("w1", [P, KD, WA], at=ada_at)
        a1 = place("a1", [P, KD, WA], at=ada_at + 2048)
        g1 = place("g1", [P, KD, GL], at=ada_at + 4096)
        gu_at = gu_hi_at
        AR = place("AR", [P, KD, TT, 2, P], at=gu_at)
        bT = place("bT", [P, KD, SEQ], at=gu_at + 16 * K1)
        kdT = place("kdT", [P, KD, SEQ], at=gu_at + 24 * K1)
        tok = place("tok", [P, 3, TT, D], at=gu_at + 32 * K1)
        U = place("U", [P, TT, D], at=gu_at + 56 * K1)
        WT = place("WT", [P, KD, SEQ], at=xT_at)
        U0 = place("U0", [P, TT, D], at=xT_at + 8192)
        cum = place("cum", [P, KD, SEQ], at=xT_at)
        decay = place("decay", [P, KD, SEQ], at=xT_at + 8192)
        kk = place("kk", [P, KD, SEQ], at=dn_at)
        keep = place("keep", [P, KD * SEQ], at=dn_at + 8 * K1)
        norm = place("norm", [P, KD, SEQ], at=dn_at + 48 * K1)
        pairs = place("pairs", [P, RH, 3, P], at=dn_at)
        inv = place("inv", [P, TT, RH, P], at=dn_at + 24 * K1)
        inv_in = place("inv_in", [P, CH, CH], at=dn_at + 40 * K1)
        inv_out = place("inv_out", [P, CH, CH], at=dn_at + 44 * K1)
        inv_tmp = place("inv_tmp", [P, CH * CH], at=dn_at + 48 * K1)
        y_tok = place("y_tok", [P, TT, D], at=dn_at + 40 * K1)
        ln = place("ln", [P, 2, D], at=dn_at + 48 * K1)
        S = place("S", [P, KD, HD], at=r0 + 16384)
        gn_sq = place("gn_sq", [P, HALF], at=r0 + 16384 + 2048)
        z_small = place("z_small", [P, TT, DSA_SMALL], at=spare_at)
        k_twice = place("k_twice", [P, KVH, 2, HD], at=junk_at)
        ik_twice = place("ik_twice", [P, TT, 2, HD], at=hid_at)
        ikT = place("ikT", [P, SEQ], at=hid_at + 1024)
        probs = place("probs", [P, 4, SEQ], at=spare_at + 640)
        probsT = place("probsT", [P, 2, 3 * P], at=spare_at + 640 + 4096)
        dstat = place("dstat", [P, 64], at=spare_at + 640 + 4096 + 3072)
        top8 = place("top8", [P, 8], at=spare_at + 640 + 4096 + 3072 + 256)
        oT = [z[:, i, 0:D].rearrange("p (j c) -> p j c", j=QH // 4) for i in range(TT)]

        bank = [ctx.enter_context(nc.psum_tensor(f"bank{i}", [P, HALF], F32)) for i in range(8)]
        acc = [[bank[0], bank[1]], [bank[2], bank[3]]]
        G = [bank[4], bank[5]]
        TB = [bank[6], bank[7]]

        consts = sem("consts")
        c_in = sem("c_in")
        h_in = sem("h_in")
        c_ready = sem("c_ready")
        raw_in = [sem("raw_in_a"), sem("raw_in_b"), sem("raw_in_down")]
        hi_ready = [sem("hi_a"), sem("hi_b"), sem("hi_down")]
        split = [sem("split_a"), sem("split_b"), sem("split_down")]
        ada_in = [sem(f"ada_in_{i}") for i in range(4)]
        bias_in = sem("bias_in")
        ada_step = sem("ada_step")
        ada_sum = sem("ada_sum")
        mods_ready = sem("mods_ready")
        g_ready = [sem("g_ready_0"), sem("g_ready_1")]
        silu_done = [sem("silu_0"), sem("silu_1")]
        hid_ready = [sem("hid_ready_0"), sem("hid_ready_1")]
        t_ready = [sem("t_ready_0"), sem("t_ready_1")]
        hT_hi_ready = [sem("hT_hi_0"), sem("hT_hi_1")]
        hT_ready = [sem("hT_ready_0"), sem("hT_ready_1")]
        d_done = [sem("d_done_0"), sem("d_done_1")]
        dve_step = sem("dve_step")
        act_step = sem("act_step")
        h_ready = sem("h_ready")
        square_sum = sem("square_sum")
        root = sem("root")
        rstd_var = sem("rstd_var")
        xn_ready = sem("xn_ready")
        xn_turned = sem("xn_turned")
        xT_hi_ready = sem("xT_hi_ready")
        xT_ready = sem("xT_ready")
        stored = sem("stored")
        gains_in = sem("gains_in")
        z_out = [sem("z_out_0"), sem("z_out_1")]
        small_normed = sem("small_normed")
        q_normed = sem("q_normed")
        k_normed = sem("k_normed")
        mean_ready = sem("mean_ready")
        mean_root = sem("mean_root")
        group_turned = sem("group_turned")
        group_out = sem("group_out")
        scores_ready = sem("scores_ready")
        relu_ready = sem("relu_ready")
        relu_used = sem("relu_used")
        score_masked = sem("score_masked")
        offset_ready = sem("offset_ready")
        offset_masked = sem("offset_masked")
        logits_ready = sem("logits_ready")
        max_ready = sem("max_ready")
        exp_ready = sem("exp_ready")
        probs_ready = sem("probs_ready")
        probs_turned = sem("probs_turned")
        probsT_ready = sem("probsT_ready")
        o_ready = sem("o_ready")
        oT_out = sem("oT_out")
        oT_hi_ready = sem("oT_hi_ready")
        oT_ready = sem("oT_ready")
        (rwkv_in, lora1_in, lora2_in, uT_ready, mix_ready, mix_hi_ready, mix_split, lora_ready, wa_hid_ready,
         wa_ready, g_out, wa_out, v_out, rc_out, kk_sq, kk_sum, kk_root, cum_ready, decay_out, ops_ready,
         rk_ready, bonus_ready, bonus_out, tok_turned, tok_out, ba_ready, ba_out, inv_saved, inv_loaded,
         inv_made, inv_stored, inv_back, pairs_mm, pairs_out, x1_ready, x1_out, u0_ready, u0_out, wt_ready, wt_out,
         u_mm, u_ready, s_mm, s_ready, ys_ready, ys_out, yg_ready, y_sum, gn_var, gn_root, m_ready, m_turned, m_hi,
         m_split, ln_in, zeroed, masks_made) = (sem(x) for x in (
             "rwkv_in", "lora1_in", "lora2_in", "uT_ready", "mix_ready", "mix_hi_ready", "mix_split", "lora_ready",
             "wa_hid_ready", "wa_ready", "g_out", "wa_out", "v_out", "rc_out", "kk_sq", "kk_sum", "kk_root",
             "cum_ready", "decay_out", "ops_ready", "rk_ready", "bonus_ready", "bonus_out", "tok_turned", "tok_out",
             "ba_ready", "ba_out", "inv_saved", "inv_loaded", "inv_made", "inv_stored", "inv_back", "pairs_mm",
             "pairs_out", "x1_ready", "x1_out", "u0_ready", "u0_out", "wt_ready", "wt_out", "u_mm", "u_ready",
             "s_mm", "s_ready", "ys_ready", "ys_out", "yg_ready", "y_sum", "gn_var", "gn_root", "m_ready",
             "m_turned", "m_hi", "m_split", "ln_in", "zeroed", "masks_made"))

        ffn_gu = a["ffn_w_gu"].rearrange("l j (k p) (g c) -> l j p k g c", p=P, g=2)
        ffn_dn = a["ffn_w_down"].rearrange("l j (t p) d -> l j p t d", p=P)
        ada_w = a["ada_w"].rearrange("l (k p) n -> l p k n", p=P)

        DSA_BLOCK0, DSA_OUT0 = 11, 16
        DSA_IN = [(2048, DSA_SMALL, lambda t: z_small[:, t, :]), (0, HALF, lambda t: z[:, t, 0:HALF]),
                  (HALF, HALF, lambda t: z[:, t, HALF:2 * HALF]), (2 * HALF, HALF, lambda t: z[:, t, 2 * HALF:3 * HALF]),
                  (3 * HALF, HALF, lambda t: z[:, t, 3 * HALF:4 * HALF])]
        GROUPS = [(0, "ik", None, 0), (1, "iq", 0, 0), (2, "iq", 1, 0), (3, "q", 0, 0), (6, "q", 0, 4), (7, "k", 0, 0),
                  (0, "k", 1, 0), (1, "q", 1, 0), (2, "q", 1, 4)]
        SCORES = [(4, 0, (0, 2, 4, 6)), (5, 0, (1, 3, 5, 7)), (3, 1, (0, 2)), (6, 1, (4, 6)), (7, 1, (1, 3)), (0, 1, (5, 7))]
        V0 = 2 * HALF + KVH * HD

        V_BLOCK, R_BLOCK, K_BLOCK, RWKV_OUT0 = 40, 42, 44, 46
        inv_dram = [nc.dram_tensor(f"inverse_{i}", [TT * 4 * RH, CH * CH], F32, kind="Internal").ap() for i in range(2)]

        g_ready_rwkv = sem("g_ready_rwkv")

        def blocks_of(f):
            n = ADA_FFN[f][1]
            if n in (0, NB):
                return [(0, 3, False), (3, 6, True), (9, 2, False)]
            return [(0, 3, False), (3, 4, True), (7, 4, False)]

        def run_blocks(eng, f, step):
            for first, count, loop in blocks_of(f):
                nv = ADA_FFN[f][1]
                if not loop:
                    for b in range(first, first + count):
                        step(b, b % 2, b < nv)
                else:
                    with eng.Fori(first, first + count - 1, 2) as b:
                        step(b, first % 2, first < nv)
                        step(b + 1, (first + 1) % 2, first < nv)

        block = ctx.enter_context(nc.Block())

        @block.sync
        def _(sp):
            x = a["x"].rearrange("b (t p) d -> p (b t) d", p=P)
            sp.dma_start(ccol[:], a["c"].rearrange("b (k p) -> p (b k)", p=P)).then_inc(c_in, 16)
            sp.wait_ge(ada_in[3], 16 * (ADA_FRONT - 1))
            sp.dma_start(h[:], x).then_inc(h_in, 16)

            def slot_free(n, i, first):
                if not first:
                    sp.wait_ge(split[i], n)

            def load_block(n, i, left, right, first=False):
                slot_free(n, i, first)
                dst = raw[:, i, :].rearrange("p (k g c) -> p k g c", k=4, g=2)
                sp.dma_start(dst[:, :, 0, :], left).then_inc(raw_in[i], 16)
                sp.dma_start(dst[:, :, 1, :], right).then_inc(raw_in[i], 16)

            def load_mixer_block(n, w, cols):
                width = cols.stop - cols.start
                for i in range(2):
                    slot_free(n, i, False)
                    dst = raw[:, i, 0:4 * width].rearrange("p (k c) -> p k c", k=4)
                    src = w.rearrange("(k p) c -> p k c", p=P)
                    for j in range(2):
                        sp.dma_start(dst[:, 2 * j:2 * j + 2, :], src[:, 4 * i + 2 * j:4 * i + 2 * j + 2, cols]
                                     ).then_inc(raw_in[i], 16)

            def dsa():
                for i, name in enumerate(("dsa_q_norm", "dsa_k_norm", "dsa_ik_norm")):
                    for e in range(2):
                        sp.dma_start(head_gain[e * HD:(e + 1) * HD, i:i + 1], a[name].rearrange("l c -> c l")
                                     ).then_inc(gains_in, 16)
                for i, (c0, width, _) in enumerate(DSA_IN):
                    load_mixer_block(DSA_BLOCK0 + i, a["dsa_w_in"][0], slice(c0, c0 + width))
                for i in range(2):
                    load_mixer_block(DSA_OUT0 + i, a["dsa_w_out"][0], slice(i * HALF, (i + 1) * HALF))

            def ffn(f):
                layer, j = divmod(f, 2)
                n0 = FFN_BLOCK0[f]

                def gate_up(b, n):
                    for i in range(2):
                        rows = ffn_gu[layer, j, :, 4 * i:4 * i + 4, :, bass.ds(b * FB, FB)]
                        load_block(n, i, rows[:, :, 0, :], rows[:, :, 1, :], isinstance(n, int) and n == 0)

                def step(b, odd, ada):
                    if isinstance(b, int) and b == 0:
                        gate_up(0, n0)
                    if isinstance(b, int) and f == 0 and b == 0:
                        sp.wait_ge(ada_in[3], 16 * ADA_FRONT)
                    if not (isinstance(b, int) and b == NB - 1):
                        gate_up(b + 1, n0 + b + 1)
                    slot_free(f * NB + b, 2, isinstance(b, int) and f * NB + b == 0)
                    sp.dma_start(raw[:, 2, :].rearrange("p (t d) -> p t d", t=2),
                                 ffn_dn[layer, j, :, bass.ds(b * 2, 2), :]).then_inc(raw_in[2], 16)
                run_blocks(sp, f, step)

            def rwkv(q):
                for i in range(6):
                    sp.dma_start(mu[:, i, :], a["rwkv_mu"][0, i:i + 1, :].rearrange("o (k p) -> p (o k)", p=P)
                                 ).then_inc(rwkv_in, 16)
                for i, name in enumerate(("rwkv_w0", "rwkv_a0", "rwkv_k_k", "rwkv_k_a")):
                    sp.dma_start(cols[:, i, :], a[name].rearrange("o (k p) -> p (o k)", p=P)).then_inc(rwkv_in, 16)
                r_k = a["rwkv_r_k"].rearrange("o (k e) c -> (o e c) k", e=2)
                sp.dma_start(cols[:, 4, :], r_k).then_inc(rwkv_in, 16)
                sp.wait_ge(ada_step, 36 * KD)
                for name, dst in (("rwkv_w1", w1), ("rwkv_a1", a1), ("rwkv_g1", g1)):
                    sp.dma_start(dst[:], a[name][0].rearrange("(k p) n -> p k n", p=P)).then_inc(lora1_in, 16)
                load_mixer_block(V_BLOCK, a["rwkv_w_rkv"][0, 2], slice(0, HALF))
                sp.wait_ge(uT_ready, 4)
                sp.dma_start(wa2[0:WA, :], a["rwkv_w2"][0]).then_inc(lora2_in, 16)
                sp.dma_start(wa2[WA:2 * WA, :], a["rwkv_a2"][0]).then_inc(lora2_in, 16)
                sp.dma_start(g2[:, 0, :], a["rwkv_g2"][0, 0:P, :]).then_inc(lora2_in, 16)
                sp.dma_start(g2[0:GL - P, 1, :], a["rwkv_g2"][0, P:GL, :]).then_inc(lora2_in, 16)
                load_mixer_block(V_BLOCK + 1, a["rwkv_w_rkv"][0, 2], slice(HALF, D))
                for j in range(2):
                    for i in range(2):
                        load_mixer_block(R_BLOCK + 2 * j + i, a["rwkv_w_rkv"][0, j], slice(i * HALF, (i + 1) * HALF))
                load_mixer_block(RWKV_OUT0, a["rwkv_w_out"][0], slice(0, HALF))
                blocks = [(t, c) for t in range(TT) for c in range(4)]

                def dram_block(i, t, c):
                    rows = slice((4 * t + c) * RH, (4 * t + c + 1) * RH)
                    return inv_dram[i][rows, :].rearrange("h (s u) -> s h u", s=CH)

                def sbuf_block(t, c):
                    return inv[c * CH:(c + 1) * CH, t, :, c * CH:(c + 1) * CH]
                sp.wait_ge(ba_out, 8)
                for t, c in blocks:
                    sp.dma_start(dram_block(0, t, c), sbuf_block(t, c)).then_inc(inv_saved, 16)
                sp.wait_ge(inv_saved, 16 * len(blocks))
                sp.wait_ge(tok_out, 12)
                sp.dma_start(inv_in[:].rearrange("p s u -> p (s u)"), inv_dram[0]).then_inc(inv_loaded, 16)
                sp.wait_ge(inv_made, 1)
                sp.dma_start(inv_dram[1], inv_out[:].rearrange("p s u -> p (s u)")).then_inc(inv_stored, 16)
                sp.wait_ge(inv_stored, 16)
                for t, c in blocks:
                    sp.dma_start(sbuf_block(t, c), dram_block(1, t, c)).then_inc(inv_back, 16)
                for i, name in enumerate(("rwkv_ln_w", "rwkv_ln_b")):
                    sp.dma_start(ln[:, i, :], a[name].broadcast_to([P, D])).then_inc(ln_in, 16)
                load_mixer_block(RWKV_OUT0 + 1, a["rwkv_w_out"][0], slice(HALF, D))

            ffn(0)
            dsa()
            ffn(1)
            ffn(2)
            rwkv(4)
            ffn(3)
            sp.wait_ge(h_ready, 4 * 6)
            sp.dma_start(out.rearrange("b (t p) d -> p (b t) d", p=P), h[:]).then_inc(stored, 16)
            sp.wait_ge(stored, 16)

        @block.gpsimd
        def _(pool):
            nc.gpsimd.memset(ident[:], 0.0).then_inc(consts, 1)
            nc.gpsimd.memset(ones[:], 1.0).then_inc(consts, 1)
            nc.gpsimd.memset(ada_bias[:], 0.0).then_inc(consts, 1)
            pool.wait_ge(consts, 3)
            nc.gpsimd.affine_select(out=ident[:], in_=ident[:], compare_op=ALU.not_equal, fill=1.0, base=0,
                                    pattern=[[-1, P]], channel_multiplier=1).then_inc(consts, 1)

            def causal(made, counts, buf, fill, masked):
                for t in range(TT):
                    pool.wait_ge(made, counts[t])
                    own = buf[:, t, t * P:(t + 1) * P]
                    nc.gpsimd.affine_select(out=own, in_=own, compare_op=ALU.is_ge, fill=fill, base=0,
                                            pattern=[[-1, P]], channel_multiplier=1).then_inc(masked, 1)

            nc.gpsimd.memset(masks[:], 1.0).then_inc(masks_made, 1)
            nc.gpsimd.memset(block_ones[:], 1.0).then_inc(masks_made, 1)
            made = {"masks": 2}

            def select(view, base, pattern, multiplier):
                pool.wait_ge(masks_made, made["masks"])
                nc.gpsimd.affine_select(out=view, in_=view, compare_op=ALU.is_ge, fill=0.0, base=base, pattern=pattern,
                                        channel_multiplier=multiplier).then_inc(masks_made, 1)
                made["masks"] += 1

            for i in range(2):
                view = masks[:, i, :].rearrange("p (c u) -> p c u", u=CH)
                select(view, 0, [[-CH, 4], [0, CH]], 1)
                select(view, CH - 1, [[CH, 4], [0, CH]], -1)
                select(view, i - 1, [[CH, 4], [1, CH]], -1)
            view = block_ones[:].rearrange("p (e c) -> p e c", e=2)
            select(view, 0, [[-HD, 2], [0, HD]], 1)
            select(view, HD - 1, [[HD, 2], [0, HD]], -1)

            causal(relu_used, (2, 6), score, NEG, score_masked)
            causal(offset_ready, (1, 2), offset, HIDDEN, offset_masked)

        @block.tensor
        def _(pe):
            def ada_total(v, spread):
                pe.wait_ge(ada_step, v * KD + KD)
                nc.tensor.matmul(spread[:], ones[:], ada_acc[:], start=True, stop=True).then_inc(ada_sum, 1)

            def turn_x(q):
                for i in range(4):
                    pe.wait_ge(xn_ready, 4 * q + i + 1)
                    for k in range(4):
                        mm = nc.tensor.transpose(bank[4 + i][:, k * P:(k + 1) * P], xn[:, i % 2, k * P:(k + 1) * P],
                                                 ident[:])
                    mm.then_inc(xn_turned, 1)

            def products(out_ap, sta_hi, sta_lo, mov_hi, mov_lo, start, stop):
                nc.tensor.matmul(out_ap, sta_hi, mov_hi, start=start, stop=False, skip_group_check=True)
                nc.tensor.matmul(out_ap, sta_hi, mov_lo, start=False, stop=False, skip_group_check=True)
                return nc.tensor.matmul(out_ap, sta_lo, mov_hi, start=False, stop=stop, skip_group_check=True)

            def gate_up(n, par, half, width=HALF):
                tok = slice(half * P, (half + 1) * P)
                for k in range(KD):
                    if half == 0 and k % 4 == 0:
                        pe.wait_ge(split[k // 4], n + 1)
                    mm = products(G[half][:, 0:width], xT_hi[:, k, tok], xT_lo[:, k, tok],
                                  gu_hi[:, par, k, 0:width], gu_lo[:, par, k, 0:width], k == 0, k == KD - 1)
                mm.then_inc(g_ready[half], 1)

            def turn_hidden(ub, half, first=False):
                pe.wait_ge(hid_ready[half], ub + 1)
                if not first:
                    pe.wait_ge(hT_ready[half], ub)
                for t in range(2):
                    mm = nc.tensor.transpose(TB[half][:, t * P:(t + 1) * P], hid[:, half, t * P:(t + 1) * P], ident[:])
                mm.then_inc(t_ready[half], 1)

            def down(ub, half, start, stop):
                pe.wait_ge(hT_ready[half], ub + 1)
                if half == 0:
                    pe.wait_ge(split[2], ub + 1)
                for t in range(2):
                    for d in range(2):
                        cols = slice(d * HALF, (d + 1) * HALF)
                        mm = products(acc[half][d][:], hT_hi[:, half, t, :], hT_lo[:, half, t, :],
                                      dn_hi[:, t, cols], dn_lo[:, t, cols], start and t == 0, stop and t == 1)
                mm.then_inc(d_done[half], 1)

            def ffn(f, q):
                turn_x(q)
                pe.wait_ge(xT_ready, 4 * (q if q < 4 else q - 1) + 4)
                n0 = FFN_BLOCK0[f]
                v0, nv = ADA_FFN[f]

                def step(b, odd, ada):
                    ub, par = f * NB + b, (n0 + odd) % 2
                    peeled = isinstance(b, int)
                    if not (peeled and b == 0):
                        pe.wait_ge(hid_ready[0], ub)
                    gate_up(n0 + b, par, 0)
                    if not (peeled and b == 0):
                        turn_hidden(ub - 1, 1, peeled and ub == 1)
                        if nv and not (peeled and b > nv):
                            pe.wait_ge(hT_ready[0], ub)
                            ada_total(v0 + b - 1, TB[0])
                        down(ub - 1, 0, peeled and b == 1, False)
                        pe.wait_ge(hid_ready[1], ub)
                    gate_up(n0 + b, par, 1)
                    if nv and not (peeled and (b == 0 or b > nv)):
                        pe.wait_ge(mods_ready, v0 + b)
                    turn_hidden(ub, 0, peeled and ub == 0)
                    if not (peeled and b == 0):
                        down(ub - 1, 1, peeled and b == 1, False)

                run_blocks(pe, f, step)
                last = f * NB + NB - 1
                turn_hidden(last, 1)
                down(last, 0, False, True)
                if nv == NB:
                    ada_total(v0 + NB - 1, TB[0])
                down(last, 1, False, True)

            def dsa(q):
                turn_x(q)
                pe.wait_ge(xT_ready, 4 * q + 4)
                for i, (_, width, _) in enumerate(DSA_IN):
                    n = DSA_BLOCK0 + i
                    for half in range(TT):
                        if i:
                            pe.wait_ge(z_out[half], i)
                        gate_up(n, n % 2, half, width)
                    if i in (0, 1, 2):
                        ada_total(15 + i, TB[(i + 1) % 2])

                def turn_group(g):
                    b, what, t, first = GROUPS[g]
                    if what == "ik":
                        pe.wait_ge(small_normed, 1)
                        tiles = [ik_twice[:, t2].rearrange("p a c -> p (a c)") for t2 in range(TT)]
                    elif what == "k":
                        pe.wait_ge(k_normed, t + 1)
                        tiles = [k_twice[:, g2].rearrange("p a c -> p (a c)") for g2 in range(KVH)]
                    else:
                        if what == "q":
                            pe.wait_ge(q_normed, t + 1)
                        else:
                            pe.wait_ge(z_out[t], 5)
                        c0 = 0 if what == "q" else 3 * HALF
                        tiles = [z[:, t, c0 + (first + j) * P:c0 + (first + j + 1) * P] for j in range(4)]
                    if b >= 6:
                        pe.wait_ge(mods_ready, 18)
                    if g >= 6:
                        pe.wait_ge(group_out, g - 5)
                    for j, tile in enumerate(tiles):
                        mm = nc.tensor.transpose(bank[b][:, j * P:(j + 1) * P], tile, ident[:])
                    mm.then_inc(group_turned, 1)

                for g in range(len(GROUPS)):
                    turn_group(g)
                pe.wait_ge(group_out, len(GROUPS))
                for b, t, heads in SCORES:
                    keys = (t + 1) * P
                    pe.wait_ge(z_out[b - 4 if b in (4, 5) else 0], 5)
                    for j, hh in enumerate(heads):
                        rows = slice(hh % 2 * HD, hh % 2 * HD + HD)
                        mm = nc.tensor.matmul(bank[b][:, j * keys:(j + 1) * keys], iqT[rows, hh // 2, t * P:(t + 1) * P],
                                              ikT[rows, 0:keys], start=True, stop=True)
                    mm.then_inc(scores_ready, 1)

                pe.wait_ge(relu_ready, len(SCORES))
                for i in range(2 * QH + 6):
                    if i < 2 * QH:
                        hh, t = divmod(i, 2)
                        rows = slice(hh % 2 * HD, hh % 2 * HD + HD)
                        if i >= 4:
                            pe.wait_ge(max_ready, i - 3)
                        nc.tensor.matmul(bank[i % 4][:, 0:(t + 1) * P], qT[rows, hh // 2, t * P:(t + 1) * P],
                                         kT[rows, hh // (QH // KVH), 0:(t + 1) * P], start=True, stop=True
                                         ).then_inc(logits_ready, 1)
                    j = i - 3
                    if 0 <= j < 2 * QH:
                        hh, t = divmod(j, 2)
                        pe.wait_ge(probs_ready, j + 1)
                        if t == 0 and hh >= 2:
                            pe.wait_ge(probsT_ready, hh - 1)
                        for s in range(t + 1):
                            mm = nc.tensor.transpose(bank[4 + hh % 2][:, (t + s) * P:(t + s + 1) * P],
                                                     probs[:, j % 4, s * P:(s + 1) * P], ident[:])
                        mm.then_inc(probs_turned, 1)
                    if i >= 6 and i % 2 == 0:
                        attend((i - 6) // 2)

                pe.wait_ge(oT_ready, 2)
                for i in range(2):
                    n = DSA_OUT0 + i
                    for half in range(TT):
                        if i:
                            pe.wait_ge(h_ready, 4 * q + half + 1)
                        gate_up(n, n % 2, half)

            def attend(hh):
                j, e = divmod(hh, 2)
                pe.wait_ge(probsT_ready, hh + 1)
                if e == 0 and j >= 2:
                    pe.wait_ge(oT_out, j - 1)
                v0 = V0 + hh // (QH // KVH) * HD
                out_rows = bank[6 + j % 2][e * HD:(e + 1) * HD, :]
                nc.tensor.matmul(out_rows[:, 0:SEQ], z[:, 0, v0:v0 + HD], probsT[:, hh % 2, 0:SEQ],
                                 start=True, stop=False, skip_group_check=True)
                nc.tensor.matmul(out_rows[:, P:SEQ], z[:, 1, v0:v0 + HD], probsT[:, hh % 2, SEQ:SEQ + P],
                                 start=False, stop=True, skip_group_check=True).then_inc(o_ready, 1)

            def rwkv(q):
                turn_x(q)
                pe.wait_ge(lora1_in, 3 * 16)
                pe.wait_ge(uT_ready, 4)
                for i, (w, out_ap) in enumerate(((w1, bank[0][0:WA, 0:SEQ]), (a1, bank[1][P - WA:P, 0:SEQ]))):
                    pe.wait_ge(mix_ready, i + 1)
                    for k in range(KD):
                        mm = nc.tensor.matmul(out_ap, w[:, k, :], mix[i][:, k, :], start=k == 0, stop=k == KD - 1)
                    mm.then_inc(lora_ready, 1)
                pe.wait_ge(mix_ready, 3)
                for i, (c0, c1) in enumerate(((0, P), (P, GL))):
                    for k in range(KD):
                        mm = nc.tensor.matmul(bank[2 + i][0:c1 - c0, 0:SEQ], g1[:, k, c0:c1], mix[2][:, k, :],
                                              start=k == 0, stop=k == KD - 1)
                    mm.then_inc(lora_ready, 1)
                pe.wait_ge(lora2_in, 4 * 16)
                pe.wait_ge(wa_hid_ready, 4)
                for m in range(KD):
                    for e in range(2):
                        rows = slice(e * WA, (e + 1) * WA)
                        mm = nc.tensor.matmul(bank[4 * e + m // 2][:, m % 2 * SEQ:(m % 2 + 1) * SEQ],
                                              wa2[rows, m * P:(m + 1) * P], hid_wa[rows, :], start=True, stop=True)
                    mm.then_inc(wa_ready, 1)
                pe.wait_ge(wa_out, 2 * KD)
                for t in range(TT):
                    ts = slice(t * P, (t + 1) * P)
                    for d in range(2):
                        ds = slice(d * HALF, (d + 1) * HALF)
                        nc.tensor.matmul(acc[t][d][:], hid_g[:, 0, ts], g2[:, 0, ds], start=True, stop=False)
                        mm = nc.tensor.matmul(acc[t][d][:], hid_g[0:GL - P, 1, ts], g2[0:GL - P, 1, ds],
                                              start=False, stop=True)
                        mm.then_inc(g_ready_rwkv, 1)
                pe.wait_ge(mix_split, 1)
                for i in range(2):
                    n = V_BLOCK + i
                    for half in range(TT):
                        if i:
                            pe.wait_ge(v_out, half + 1)
                        gate_up(n, n % 2, half)
                for i in range(4):
                    n = R_BLOCK + i
                    pe.wait_ge(mix_split, 2 + i // 2)
                    for half in range(2):
                        if i:
                            pe.wait_ge(rc_out, 2 * i + half - 1)
                        else:
                            pe.wait_ge(v_out, 3 + half)
                        if half == 0:
                            for k in range(2):
                                pe.wait_ge(split[k], n + 1)
                        for m in range(2 * half, 2 * half + 2):
                            ms = slice(m * P, (m + 1) * P)
                            for k in range(KD):
                                mm = products(G[half][:, m % 2 * SEQ:(m % 2 + 1) * SEQ], gu_hi[:, n % 2, k, ms],
                                              gu_lo[:, n % 2, k, ms], xT_hi[:, k, :], xT_lo[:, k, :],
                                              k == 0, k == KD - 1)
                        mm.then_inc(g_ready[half], 1)
                pe.wait_ge(masks_made, 10)
                pe.wait_ge(kk_sq, 1)
                for i in range(4):
                    nc.tensor.matmul(bank[i][:], block_ones[:], norm[:, 2 * i:2 * i + 2, :].rearrange("p k c -> p (k c)"),
                                     start=True, stop=True).then_inc(kk_sum, 1)
                pe.wait_ge(rk_ready, 1)
                for t in range(TT):
                    for k in range(KD):
                        mm = nc.tensor.matmul(bank[4][:, t * RH + 2 * k:t * RH + 2 * k + 2],
                                              norm[:, k, t * P:(t + 1) * P], rk_heads[:, k, :], start=True, stop=True)
                mm.then_inc(bonus_ready, 1)
                pe.wait_ge(ops_ready, 2)
                for i in range(8):
                    t, h0 = divmod(i, 4)
                    b = 2 * (h0 % 2)
                    if i >= 2:
                        pe.wait_ge(ba_out, i - 1)
                    for j in range(4):
                        hh = 8 * (h0 // 2) + 2 * j + h0 % 2
                        rows = slice(hh % 2 * HD, hh % 2 * HD + HD)
                        mm = nc.tensor.matmul(bank[b][:, j * P:(j + 1) * P], bT[rows, hh // 2, t * P:(t + 1) * P],
                                              AR[rows, hh // 2, t, 0, :], start=True, stop=True)
                    mm.then_inc(ba_ready, 1)
                pe.wait_ge(ops_ready, 4)
                pe.wait_ge(bonus_out, 1)
                srcs = [lambda k, t: AR[:, k, t, 0, :], lambda k, t: bT[:, k, t * P:(t + 1) * P],
                        lambda k, t: kdT[:, k, t * P:(t + 1) * P]]
                for i in range(12):
                    what, t, d = i // 4, i // 2 % 2, i % 2
                    if i >= 3:
                        pe.wait_ge(tok_out, i - 2)
                    for j in range(4):
                        mm = nc.tensor.transpose(bank[5 + i % 3][:, j * P:(j + 1) * P], srcs[what](4 * d + j, t), ident[:])
                    mm.then_inc(tok_turned, 1)

                def pairs_of(t):
                    for hh in range(RH):
                        rows = slice(hh % 2 * HD, hh % 2 * HD + HD)
                        n = t * RH + hh
                        b = bank[(0, 4)[hh % 2] + hh // 2 % 2]
                        if n >= 4:
                            pe.wait_ge(pairs_out, n - 3)
                        ts = slice(t * P, (t + 1) * P)
                        nc.tensor.matmul(b[:, 0:P], bT[rows, hh // 2, ts], AR[rows, hh // 2, t, 1, :],
                                         start=True, stop=True)
                        nc.tensor.matmul(b[:, P:3 * P], kdT[rows, hh // 2, ts],
                                         AR[rows, hh // 2, t].rearrange("p a c -> p (a c)"),
                                         start=True, stop=True).then_inc(pairs_mm, 1)

                def by_head(t, sta, mov, banks, sem_out):
                    for hh in range(RH):
                        mm = nc.tensor.matmul(banks[hh // 8][:, hh % 8 * HD:(hh % 8 + 1) * HD], sta(hh), mov(hh),
                                              start=True, stop=True)
                        if hh % 8 == 7:
                            mm.then_inc(sem_out, 1)

                pe.wait_ge(ba_out, 8)
                pe.wait_ge(tok_out, 12)
                for t in range(TT):
                    if t:
                        pe.wait_ge(y_sum, 2)
                    pairs_of(t)
                    hs = lambda hh: slice(hh * HD, (hh + 1) * HD)
                    pe.wait_ge(pairs_out, RH * (t + 1))
                    by_head(t, lambda hh: pairs[:, hh, 1, :], lambda hh: v_tok[:, t, hs(hh)], [bank[6], bank[7]], x1_ready)
                    pe.wait_ge(inv_back, 8 * 16)
                    pe.wait_ge(x1_out, 2 * t + 2)
                    by_head(t, lambda hh: inv[:, t, hh, :], lambda hh: U[:, t, hs(hh)], [bank[6], bank[7]], u0_ready)
                    for hh in range(RH):
                        e, j = hh % 2, hh // 2
                        mm = nc.tensor.matmul(bank[2 + j // 4][e * HD:(e + 1) * HD, j % 4 * P:(j % 4 + 1) * P],
                                              tok[:, 0, t, hs(hh)], inv[:, t, hh, :], start=True, stop=True)
                        if hh % 8 == 7:
                            mm.then_inc(wt_ready, 1)
                    pe.wait_ge(u0_out, 2 * t + 2)
                    pe.wait_ge(wt_out, 2 * t + 2)
                    for cc in range(4):
                        c = 4 * t + cc
                        rows = slice(cc * CH, (cc + 1) * CH)
                        sb_ = bank[2 + c % 2]
                        if c >= 2:
                            pe.wait_ge(s_ready, c - 1)
                        for hh in range(RH):
                            e, j = hh % 2, hh // 2
                            nc.tensor.matmul(sb_[e * HD:(e + 1) * HD, j * HD:(j + 1) * HD], tok[rows, 2, t, hs(hh)],
                                             v_tok[rows, t, hs(hh)], start=j == 0, stop=False, skip_group_check=True,
                                             tile_position=(cc * CH, e * HD))
                        if c:
                            pe.wait_ge(s_ready, c)
                        ts = slice(c * CH, (c + 1) * CH)
                        for e in range(2):
                            hr = slice(e * HD, (e + 1) * HD)
                            for j in range(KD):
                                mm = nc.tensor.matmul(bank[e][rows, j * HD:(j + 1) * HD], WT[hr, j, ts], S[hr, j, :],
                                                      start=True, stop=True, tile_position=(e * HD, cc * CH))
                            mm.then_inc(u_mm, 1)
                        for e in range(2):
                            hr = slice(e * HD, (e + 1) * HD)
                            for j in range(KD):
                                mm = nc.tensor.matmul(bank[4 + e][rows, j * HD:(j + 1) * HD],
                                                      AR[hr, j, t, 1, cc * CH:(cc + 1) * CH], S[hr, j, :],
                                                      start=True, stop=True, tile_position=(e * HD, cc * CH))
                        mm.then_inc(ys_ready, 1)
                        pe.wait_ge(u_ready, 2 * c + 2)
                        for hh in range(RH):
                            e, j = hh % 2, hh // 2
                            mm = nc.tensor.matmul(sb_[e * HD:(e + 1) * HD, j * HD:(j + 1) * HD], tok[rows, 1, t, hs(hh)],
                                                  U[rows, t, hs(hh)], start=False, stop=j == KD - 1,
                                                  skip_group_check=True, tile_position=(cc * CH, e * HD))
                        mm.then_inc(s_mm, 1)
                    for hh in range(RH):
                        out_ap = bank[6 + hh // 8][:, hh % 8 * HD:(hh % 8 + 1) * HD]
                        nc.tensor.matmul(out_ap, pairs[:, hh, 0, :], U[:, t, hs(hh)], start=True, stop=False)
                        mm = nc.tensor.matmul(out_ap, pairs[:, hh, 2, :], v_tok[:, t, hs(hh)], start=False, stop=True)
                        if hh % 8 == 7:
                            mm.then_inc(yg_ready, 1)
                for i in range(4):
                    pe.wait_ge(m_ready, i + 1)
                    t, d = divmod(i, 2)
                    for k in range(4):
                        mm = nc.tensor.transpose(bank[i][:, k * P:(k + 1) * P],
                                                 y_tok[:, t, (4 * d + k) * P:(4 * d + k + 1) * P], ident[:])
                    mm.then_inc(m_turned, 1)
                pe.wait_ge(m_split, 4)
                for i in range(2):
                    n = RWKV_OUT0 + i
                    for half in range(TT):
                        if i:
                            pe.wait_ge(h_ready, 4 * q + half + 1)
                        gate_up(n, n % 2, half)

            pe.wait_ge(consts, 4)
            for v in range(ADA_FRONT):
                if v >= 2:
                    pe.wait_ge(mods_ready, v - 1)
                ada_total(v, TB[v % 2])
            ffn(0, 0)
            dsa(1)
            ffn(1, 2)
            ffn(2, 3)
            rwkv(4)
            ffn(3, 5)

        @block.scalar
        def _(act):
            def load_ada(v, layer, hv, first=False):
                if not first:
                    act.wait_ge(ada_step, v * KD - KD + 1)
                act.dma_start(ada_bias[0:1, :], a["ada_b"][layer:layer + 1, bass.ds(hv * HALF, HALF)]
                              ).then_inc(bias_in, 16)
                for i in range(4):
                    if not first:
                        act.wait_ge(ada_step, v * KD + 2 * i - 6)
                    act.dma_start(ada_raw[:, i], ada_w[layer, :, 2 * i:2 * i + 2, bass.ds(hv * HALF, HALF)]
                                  ).then_inc(ada_in[i], 16)

            def copy_mods(v, hv, spread):
                act.wait_ge(ada_sum, v + 1)
                nc.scalar.copy(mods[:, bass.ds(hv, 1), :].rearrange("p a n -> p (a n)"), spread[:]).then_inc(mods_ready, 1)

            def round_block(n, par, first=False, width=HALF):
                if not first:
                    act.wait_ge(g_ready[1], n - 1)
                for i in range(2):
                    act.wait_ge(raw_in[i], 32 * n + 32)
                    nc.scalar.copy(gu_hi[:, par, 4 * i:4 * i + 4, 0:width],
                                   raw[:, i, 0:4 * width].rearrange("p (k c) -> p k c", k=4)).then_inc(hi_ready[i], 1)

            def round_down(ub, first):
                if not first:
                    act.wait_ge(d_done[1], ub)
                act.wait_ge(raw_in[2], 16 * ub + 16)
                nc.scalar.copy(dn_hi[:], raw[:, 2, :].rearrange("p (t d) -> p t d", t=2)
                               ).then_inc(hi_ready[2], 1)

            def silu(n, ub, half, first=False):
                act.wait_ge(g_ready[half], n + 1)
                if not first:
                    act.wait_ge(t_ready[half], ub)
                nc.scalar.activation(hid[:, half, :], G[half][:, 0:FB], ACT.Silu).then_inc(silu_done[half], 1)

            def round_hidden(ub, half, first=False):
                act.wait_ge(t_ready[half], ub + 1)
                if not first:
                    act.wait_ge(d_done[half], ub)
                nc.scalar.copy(hT_hi[:, half], TB[half][:, 0:2 * P].rearrange("p (t c) -> p t c", t=2)
                               ).then_inc(hT_hi_ready[half], 1)

            def squares_of_h(q):
                act.wait_ge(h_in, 16)
                if q:
                    act.wait_ge(h_ready, 4 * q)
                for t in range(TT):
                    if t:
                        act.wait_ge(square_sum, TT * q + t)
                    nc.scalar.activation(junk[:], h[:, t, :], ACT.Square,
                                         accum_out=stat[:, t:t + 1]).then_inc(square_sum, 1)

            def modulate(q, plain=False, squares_taken=False):
                if not squares_taken:
                    squares_of_h(q)
                act.wait_ge(rstd_var, q + 1)
                nc.scalar.activation(stat[:, 4:6], stat[:, 2:4], ACT.Sqrt).then_inc(root, 1)
                for i in range(4):
                    act.wait_ge(xn_turned, 4 * q + i + 1)
                    if plain:
                        nc.scalar.copy(uT[:, 4 * (i % 2):4 * (i % 2) + 4, (i // 2) * P:(i // 2 + 1) * P],
                                       bank[4 + i][:].rearrange("p (k c) -> p k c", k=4)).then_inc(uT_ready, 1)
                        continue
                    nc.scalar.copy(xT_hi[:, 4 * (i % 2):4 * (i % 2) + 4, (i // 2) * P:(i // 2 + 1) * P],
                                   bank[4 + i][:].rearrange("p (k c) -> p k c", k=4)).then_inc(xT_hi_ready, 1)

            def dsa(q):
                def round_in(i):
                    n = DSA_BLOCK0 + i
                    round_block(n, n % 2, width=DSA_IN[i][1] if i < len(DSA_IN) else HALF)

                round_in(0)
                load_ada(15, 0, 15)
                modulate(q)
                round_in(1)
                for i, (_, width, dst) in enumerate(DSA_IN):
                    for half in range(TT):
                        act.wait_ge(g_ready[half], DSA_BLOCK0 + i + 1)
                        nc.scalar.copy(dst(half), G[half][:, 0:width]).then_inc(z_out[half], 1)
                    round_in(i + 2)
                    if i in (0, 1, 2):
                        copy_mods(15 + i, 15 + i, TB[(i + 1) % 2])
                    if i in (0, 1):
                        load_ada(16 + i, 0, 16 + i)
                    if i:
                        roots = {1: (0, 2), 2: (16, 16 + 2 * QH), 3: (4, 4 + 2 * KVH)}.get(i)
                        if roots:
                            r = dstat[:, roots[0]:roots[1]]
                            act.wait_ge(mean_ready, i)
                            nc.scalar.activation(r, r, ACT.Sqrt).then_inc(mean_root, 1)

                act.wait_ge(gains_in, 6 * 16)
                for g, (b, what, t, first) in enumerate(GROUPS):
                    act.wait_ge(group_turned, g + 1)
                    gain = {"q": 0, "k": 1, "ik": 2, "iq": None}[what]
                    src = bank[b][:].rearrange("p (j c) -> p j c", j=4)
                    if what == "ik":
                        dst, src = ikT[:], bank[b][:, 0:SEQ]
                    elif what == "q":
                        dst = qT[:, first:first + 4, t * P:(t + 1) * P]
                    else:
                        dst = (kT if what == "k" else iqT)[:, :, t * P:(t + 1) * P]
                    if gain is None:
                        nc.scalar.copy(dst, src).then_inc(group_out, 1)
                    else:
                        nc.scalar.activation(dst, src, ACT.Copy, scale=head_gain[:, gain:gain + 1]).then_inc(group_out, 1)
                for i, (b, _, _) in enumerate(SCORES):
                    act.wait_ge(scores_ready, i + 1)
                    act.wait_ge(k_normed, TT)
                    if i >= 2:
                        act.wait_ge(relu_used, i - 1)
                    nc.scalar.activation(relu[:, i % 2, :], bank[b][:], ACT.Relu).then_inc(relu_ready, 1)
                for i in range(2 * QH + 1):
                    if i < 2 * QH:
                        t = i % 2
                        act.wait_ge(max_ready, i + 1)
                        nc.scalar.activation(probs[:, i % 4, 0:(t + 1) * P], probs[:, i % 4, 0:(t + 1) * P], ACT.Exp,
                                             bias=dstat[:, 8 + i % 4:9 + i % 4],
                                             accum_out=dstat[:, 12 + i % 4:13 + i % 4]).then_inc(exp_ready, 1)
                    if i >= 4 and i % 2 == 0:
                        turned_probs(i // 2 - 2)
                for hh in range(QH - 1, QH):
                    turned_probs(hh)
                act.wait_ge(oT_out, QH // 2)
                for i in range(2):
                    ks = slice(4 * i, 4 * i + 4)
                    nc.scalar.copy(xT_hi[:, ks, :], oT[i]).then_inc(oT_hi_ready, 1)

            def turned_probs(hh):
                act.wait_ge(probs_turned, 2 * hh + 2)
                if hh >= 2:
                    act.wait_ge(o_ready, hh - 1)
                nc.scalar.copy(probsT[:, hh % 2, :], bank[4 + hh % 2][:, 0:3 * P]).then_inc(probsT_ready, 1)

            def rwkv(q):
                def r_in(n):
                    round_block(n, n % 2)

                r_in(V_BLOCK)
                modulate(q, plain=True)
                for i, (dst, src, fn) in enumerate((
                        (hid_wa[0:WA, :], bank[0][0:WA, 0:SEQ], ACT.Tanh),
                        (hid_wa[P - WA:P, :], bank[1][P - WA:P, 0:SEQ], ACT.Copy),
                        (hid_g[:, 0, :], bank[2][:, 0:SEQ], ACT.Sigmoid),
                        (hid_g[0:GL - P, 1, :], bank[3][0:GL - P, 0:SEQ], ACT.Sigmoid))):
                    act.wait_ge(lora_ready, i + 1)
                    nc.scalar.activation(dst, src, fn).then_inc(wa_hid_ready, 1)
                act.wait_ge(rwkv_in, 11 * 16)
                for m in range(KD):
                    act.wait_ge(wa_ready, m // 2 * 2 + 2)
                    for e, dst in ((0, sigT), (1, aT)):
                        nc.scalar.activation(dst[:, m, :], bank[4 * e + m // 2][:, m % 2 * SEQ:(m % 2 + 1) * SEQ],
                                             ACT.Sigmoid, bias=cols[:, e, m:m + 1]).then_inc(wa_out, 1)
                r_in(V_BLOCK + 1)

                def round_mix(i):
                    act.wait_ge(mix_ready, 4 + i)
                    if i:
                        act.wait_ge(g_ready[1], V_BLOCK + 2 * i)
                    else:
                        act.wait_ge(lora_ready, 4)
                    for half in range(2):
                        ks = slice(4 * half, 4 * half + 4)
                        nc.scalar.copy(xT_hi[:, ks, :], mix[2][:, ks, :]).then_inc(mix_hi_ready, 1)

                round_mix(0)
                for t in range(TT):
                    for d in range(2):
                        act.wait_ge(g_ready_rwkv, 2 * t + d + 1)
                        nc.scalar.copy(g_tok[:, t, d * HALF:(d + 1) * HALF], acc[t][d][:]).then_inc(g_out, 1)
                for i in range(2):
                    for half in range(TT):
                        act.wait_ge(g_ready[half], V_BLOCK + i + 1)
                        nc.scalar.copy(v_tok[:, half, i * HALF:(i + 1) * HALF], G[half][:]).then_inc(v_out, 1)
                    r_in(R_BLOCK + i)
                for i in range(4):
                    if i % 2 == 0:
                        round_mix(1 + i // 2)
                    dst = rT if i < 2 else kTc
                    for half in range(2):
                        act.wait_ge(g_ready[half], R_BLOCK + i + 1)
                        k0 = 4 * (i % 2) + 2 * half
                        nc.scalar.copy(dst[:, k0:k0 + 2, :], G[half][:].rearrange("p (k c) -> p k c", k=2)
                                       ).then_inc(rc_out, 1)
                    if i < 2:
                        r_in(K_BLOCK + i)
                act.wait_ge(cum_ready, 1)
                nc.scalar.activation(decay[:], cum[:], ACT.Exp, scale=-DECAY).then_inc(decay_out, 1)
                act.wait_ge(cum_ready, 2)
                nc.scalar.activation(decay[:], decay[:], ACT.Exp, scale=-DECAY).then_inc(decay_out, 1)
                for i in range(4):
                    act.wait_ge(kk_sum, i + 1)
                    nc.scalar.activation(sigT[:, 2 * i:2 * i + 2, :], bank[i][:].rearrange("p (k c) -> p k c", k=2),
                                         ACT.Sqrt).then_inc(kk_root, 1)
                act.wait_ge(cum_ready, 3)
                nc.scalar.activation(decay[:], cum[:], ACT.Exp, scale=DECAY).then_inc(decay_out, 1)
                act.wait_ge(bonus_ready, 1)
                nc.scalar.copy(rstat[:, 0:2 * RH], bank[4][:, 0:2 * RH]).then_inc(bonus_out, 1)
                for i in range(12):
                    what, t, d = i // 4, i // 2 % 2, i % 2
                    act.wait_ge(tok_turned, i + 1)
                    nc.scalar.copy(tok[:, what, t, d * HALF:(d + 1) * HALF], bank[5 + i % 3][:]).then_inc(tok_out, 1)
                for t in range(TT):
                    for d in range(2):
                        act.wait_ge(x1_ready, 2 * t + d + 1)
                        nc.scalar.copy(U[:, t, d * HALF:(d + 1) * HALF], bank[6 + d][:]).then_inc(x1_out, 1)
                    for d in range(2):
                        act.wait_ge(u0_ready, 2 * t + d + 1)
                        nc.scalar.copy(U0[:, t, d * HALF:(d + 1) * HALF], bank[6 + d][:]).then_inc(u0_out, 1)
                    for d in range(2):
                        act.wait_ge(wt_ready, 2 * t + d + 1)
                        nc.scalar.copy(WT[:, 4 * d:4 * d + 4, t * P:(t + 1) * P],
                                       bank[2 + d][:].rearrange("p (k c) -> p k c", k=4)).then_inc(wt_out, 1)
                    act.wait_ge(ys_ready, 4 * t + 4)
                    for e in range(2):
                        nc.scalar.copy(y_tok[:, t, :].rearrange("p (j e c) -> p j e c", e=2, c=HD)[:, :, e, :],
                                       bank[4 + e][:].rearrange("p (j c) -> p j c", c=HD)).then_inc(ys_out, 1)
                    act.wait_ge(gn_var, t + 1)
                    nc.scalar.activation(rstat[:, 48:48 + RH], rstat[:, 32:32 + RH], ACT.Sqrt).then_inc(gn_root, 1)
                act.wait_ge(yg_ready, 4)
                for i in range(2):
                    n = RWKV_OUT0 + i
                    for half in range(2):
                        act.wait_ge(raw_in[half], 32 * n + 32)
                        nc.scalar.copy(gu_hi[:, n % 2, 4 * half:4 * half + 4, :],
                                       raw[:, half, :].rearrange("p (k c) -> p k c", k=4)).then_inc(hi_ready[half], 1)
                for i in range(4):
                    act.wait_ge(m_turned, i + 1)
                    t, d = divmod(i, 2)
                    nc.scalar.copy(xT_hi[:, 4 * d:4 * d + 4, t * P:(t + 1) * P],
                                   bank[i][:].rearrange("p (k c) -> p k c", k=4)).then_inc(m_hi, 1)

            def ffn(f, q=None):
                if q is not None:
                    round_block(FFN_BLOCK0[f], FFN_BLOCK0[f] % 2)
                    modulate(q)
                n0 = FFN_BLOCK0[f]
                v0, nv = ADA_FFN[f]

                def step(b, odd, ada):
                    ub, n = f * NB + b, n0 + b
                    peeled = isinstance(b, int)
                    if not (peeled and b == 0):
                        silu(n - 1, ub - 1, 1, peeled and ub == 1)
                        round_hidden(ub - 1, 0, peeled and ub == 1)
                        round_down(ub - 1, peeled and ub == 1)
                    if ada:
                        load_ada(v0 + b, v0 // HV, v0 % HV + b)
                    if not (peeled and b == NB - 1):
                        round_block(n + 1, (n0 + odd + 1) % 2, peeled and n == 0)
                    silu(n, ub, 0, peeled and ub == 0)
                    if not (peeled and b == 0):
                        round_hidden(ub - 1, 1, peeled and ub == 1)
                        if nv and not (peeled and b > nv):
                            copy_mods(v0 + b - 1, v0 % HV + b - 1, TB[0])

                run_blocks(act, f, step)
                last = f * NB + NB - 1
                silu(n0 + NB - 1, last, 1)
                round_hidden(last, 0)
                round_down(last, False)
                round_hidden(last, 1)
                if nv == NB:
                    copy_mods(v0 + NB - 1, v0 % HV + NB - 1, TB[0])

            act.wait_ge(c_in, 16)
            nc.scalar.activation(cact[:], ccol[:], ACT.Silu).then_inc(c_ready, 1)
            act.wait_ge(consts, 4)
            for v in range(ADA_FRONT):
                load_ada(v, 0, v, v == 0)
                if v:
                    copy_mods(v - 1, v - 1, TB[(v - 1) % 2])
            squares_of_h(0)
            copy_mods(ADA_FRONT - 1, ADA_FRONT - 1, TB[(ADA_FRONT - 1) % 2])
            round_block(0, 0, True)
            modulate(0, squares_taken=True)
            ffn(0)
            dsa(1)
            ffn(1, 2)
            ffn(2, 3)
            rwkv(4)
            ffn(3, 5)

        @block.vector
        def _(dve):
            count = {"step": 0, "root": 0}

            def chain(ins):
                count["step"] += 1
                ins.then_inc(dve_step, 1)
                dve.wait_ge(dve_step, count["step"])

            def ada_products(v, first=False):
                dve.wait_ge(bias_in, 16 * v + 16)
                if not first:
                    dve.wait_ge(ada_sum, v)
                for k in range(KD):
                    if k % 2 == 0:
                        dve.wait_ge(ada_in[k // 2], 16 * v + 16)
                    if k:
                        dve.wait_ge(ada_step, v * KD + k)
                    nc.vector.scalar_tensor_tensor(out=ada_acc[:], in0=ada_raw[:, k // 2, k % 2, :],
                                                   scalar=cact[:, k:k + 1], in1=ada_acc[:] if k else ada_bias[:],
                                                   op0=ALU.mult, op1=ALU.add).then_inc(ada_step, 1)

            def rest_of_block(n, par, width=HALF):
                for i in range(2):
                    ks = slice(4 * i, 4 * i + 4)
                    dve.wait_ge(hi_ready[i], n + 1)
                    nc.vector.tensor_tensor(gu_lo[:, par, ks, 0:width],
                                            raw[:, i, 0:4 * width].rearrange("p (k c) -> p k c", k=4),
                                            gu_hi[:, par, ks, 0:width].bitcast(F32), ALU.subtract).then_inc(split[i], 1)

            def rest_of_down(ub):
                dve.wait_ge(hi_ready[2], ub + 1)
                nc.vector.tensor_tensor(dn_lo[:], raw[:, 2, :].rearrange("p (t d) -> p t d", t=2),
                                        dn_hi[:].bitcast(F32), ALU.subtract).then_inc(split[2], 1)

            def times_up(ub, half):
                dve.wait_ge(silu_done[half], ub + 1)
                nc.vector.tensor_tensor(hid[:, half, :], hid[:, half, :], G[half][:, FB:2 * FB], ALU.mult
                                        ).then_inc(hid_ready[half], 1)

            def rest_of_hidden(ub, half):
                dve.wait_ge(hT_hi_ready[half], ub + 1)
                nc.vector.tensor_tensor(hT_lo[:, half], TB[half][:, 0:2 * P].rearrange("p (t c) -> p t c", t=2),
                                        hT_hi[:, half].bitcast(F32), ALU.subtract).then_inc(hT_ready[half], 1)

            def modulate(q, shift, scale, mods_made, plain=False):
                dve.wait_ge(square_sum, TT * (q + 1))
                nc.vector.tensor_scalar(stat[:, 2:4], stat[:, 0:2], 1.0 / D, RMS_EPS, ALU.mult, ALU.add
                                        ).then_inc(rstd_var, 1)
                dve.wait_ge(root, q + 1)
                chain(nc.vector.reciprocal(stat[:, 6:8], stat[:, 4:6]))
                dve.wait_ge(mods_ready, mods_made)
                for i in range(4):
                    t, d = divmod(i, 2)
                    if i >= 2:
                        dve.wait_ge(xn_turned, 4 * q + i - 1)
                    chain(nc.vector.scalar_tensor_tensor(out=xn[:, d], in0=mods[:, 2 * scale + d], scalar=1.0,
                                                         in1=h[:, t, d * HALF:(d + 1) * HALF], op0=ALU.add, op1=ALU.mult))
                    nc.vector.scalar_tensor_tensor(out=xn[:, d], in0=xn[:, d], scalar=stat[:, 6 + t:7 + t],
                                                   in1=mods[:, 2 * shift + d], op0=ALU.mult, op1=ALU.add
                                                   ).then_inc(xn_ready, 1)
                if plain:
                    return
                made = 4 * (q if q < 4 else q - 1)
                for i in range(4):
                    t, d = divmod(i, 2)
                    dve.wait_ge(xT_hi_ready, made + i + 1)
                    part = (slice(None), slice(4 * d, 4 * d + 4), slice(t * P, (t + 1) * P))
                    nc.vector.tensor_tensor(xT_lo[part], bank[4 + i][:].rearrange("p (k c) -> p k c", k=4),
                                            xT_hi[part].bitcast(F32), ALU.subtract).then_inc(xT_ready, 1)

            def residual(q, gate, factor, mods_made):
                dve.wait_ge(mods_ready, mods_made)
                for i in range(4):
                    t, d = divmod(i, 2)
                    cols = slice(d * HALF, (d + 1) * HALF)
                    chain(nc.vector.scalar_tensor_tensor(out=xn[:, d], in0=acc[t][d][:], scalar=factor,
                                                         in1=mods[:, 2 * gate + d], op0=ALU.mult, op1=ALU.mult))
                    nc.vector.tensor_tensor(h[:, t, cols], h[:, t, cols], xn[:, d], ALU.add).then_inc(h_ready, 1)

            def rwkv(q):
                def rest_in(n):
                    rest_of_block(n, n % 2)

                rest_in(V_BLOCK)
                dve.wait_ge(rwkv_in, 11 * 16)
                chain(nc.vector.memset(rk_heads[:], 0.0))
                for e in range(2):
                    rows = slice(e * HD, (e + 1) * HD)
                    nc.vector.tensor_copy(rk_heads[rows, :, e], cols[rows, 4, :]).then_inc(zeroed, 1)
                modulate(q, 3, 4, 36, plain=True)
                dve.wait_ge(uT_ready, 4)
                nc.vector.tensor_tensor(xxT[:, :, 1:SEQ], uT[:, :, 0:SEQ - 1], uT[:, :, 1:SEQ], ALU.subtract
                                        ).then_inc(zeroed, 1)
                nc.vector.tensor_scalar(xxT[:, :, 0:1], uT[:, :, 0:1], -1.0, None, ALU.mult).then_inc(zeroed, 1)
                dve.wait_ge(zeroed, 4)

                def mix_in(i, dst):
                    for k in range(KD):
                        ins = nc.vector.scalar_tensor_tensor(out=dst[:, k, :], in0=xxT[:, k, :], scalar=mu[:, i, k:k + 1],
                                                             in1=uT[:, k, :], op0=ALU.mult, op1=ALU.add)
                    ins.then_inc(mix_ready, 1)

                def rest_of_mix(i):
                    for half in range(2):
                        ks = slice(4 * half, 4 * half + 4)
                        dve.wait_ge(mix_hi_ready, 2 * i + half + 1)
                        ins = nc.vector.tensor_tensor(xT_lo[:, ks, :], mix[2][:, ks, :], xT_hi[:, ks, :].bitcast(F32),
                                                      ALU.subtract)
                    ins.then_inc(mix_split, 1)

                mix_in(3, mix[0])
                mix_in(4, mix[1])
                mix_in(5, mix[2])
                dve.wait_ge(lora_ready, 4)
                mix_in(2, mix[2])
                rest_of_mix(0)
                rest_in(V_BLOCK + 1)
                dve.wait_ge(mix_split, 1)
                mix_in(0, mix[2])
                dve.wait_ge(wa_out, 2 * KD)
                rest_in(R_BLOCK)
                rest_in(R_BLOCK + 1)
                rest_of_mix(1)
                dve.wait_ge(mix_split, 2)
                mix_in(1, mix[2])
                rest_in(K_BLOCK)
                rest_in(K_BLOCK + 1)
                rest_of_mix(2)
                dve.wait_ge(mix_split, 3)
                chain(nc.vector.memset(keep[:], 1.0))
                chain(nc.vector.memset(keep[:].rearrange("p (n c) -> p n c", c=CH)[:, :, 0:1], 0.0))
                dve.wait_ge(g_ready[1], RWKV_OUT0)
                flat = [x[:].rearrange("p k c -> p (k c)") for x in (cum, sigT, decay)]
                nc.vector.tensor_tensor_scan(flat[0], keep[:], flat[1], 0.0, ALU.mult, ALU.add).then_inc(cum_ready, 1)
                dve.wait_ge(rc_out, 8)
                for k in range(KD):
                    ins = nc.vector.tensor_scalar(kk[:, k, :], kTc[:, k, :], cols[:, 2, k:k + 1], None, ALU.mult)
                chain(ins)
                nc.vector.tensor_tensor(norm[:], kk[:], kk[:], ALU.mult).then_inc(kk_sq, 1)
                dve.wait_ge(decay_out, 1)
                parts = lambda x: x[:].rearrange("p k (t c) -> p k t c", t=TT)
                for t in range(TT):
                    ins = nc.vector.tensor_tensor(AR[:, :, t, 1, :], parts(rT)[:, :, t, :], parts(decay)[:, :, t, :],
                                                  ALU.mult)
                chain(ins)
                nc.vector.tensor_copy(chunk_decay[:], decay[:].rearrange("p k (n c) -> p k n c", c=CH)[:, :, :, CH - 1]
                                      ).then_inc(ops_ready, 1)
                dve.wait_ge(ops_ready, 1)
                nc.vector.tensor_tensor(decay[:], cum[:], sigT[:], ALU.subtract).then_inc(cum_ready, 1)
                dve.wait_ge(kk_root, 4)
                chain(nc.vector.tensor_scalar(sigT[:], sigT[:], 1e-12, None, ALU.max))
                chain(nc.vector.reciprocal(sigT[:], sigT[:]))
                chain(nc.vector.tensor_tensor(kk[:], kk[:], sigT[:], ALU.mult))
                dve.wait_ge(decay_out, 2)
                for t in range(TT):
                    ins = nc.vector.scalar_tensor_tensor(out=AR[:, :, t, 0, :], in0=parts(kk)[:, :, t, :], scalar=-1.0,
                                                         in1=parts(decay)[:, :, t, :], op0=ALU.mult, op1=ALU.mult)
                ins.then_inc(cum_ready, 1)
                dve.wait_ge(cum_ready, 3)
                chain(nc.vector.tensor_tensor(kk[:], kk[:], aT[:], ALU.mult))
                for k in range(KD):
                    ins = nc.vector.tensor_scalar(aT[:, k, :], aT[:, k, :], -1.0, cols[:, 3, k:k + 1], ALU.add, ALU.mult)
                chain(ins)
                chain(nc.vector.scalar_tensor_tensor(out=kTc[:], in0=aT[:], scalar=1.0, in1=kTc[:], op0=ALU.add,
                                                     op1=ALU.mult))
                dve.wait_ge(decay_out, 3)
                nc.vector.tensor_tensor(bT[:], kk[:], decay[:], ALU.mult).then_inc(ops_ready, 1)
                nc.vector.tensor_tensor(kdT[:], kTc[:], decay[:], ALU.mult).then_inc(ops_ready, 1)
                nc.vector.tensor_tensor(norm[:], rT[:], kTc[:], ALU.mult).then_inc(rk_ready, 1)
                dve.wait_ge(rk_ready, 1)
                dve.wait_ge(g_out, 4)
                nc.vector.memset(S[:], 0.0).then_inc(ops_ready, 1)
                dve.wait_ge(masks_made, 10)
                for i in range(8):
                    t, h0 = divmod(i, 4)
                    dve.wait_ge(ba_ready, i + 1)
                    dst = inv[:, t].rearrange("p (g j e) c -> p g j e c", g=2, e=2)[:, h0 // 2, :, h0 % 2, :]
                    nc.vector.tensor_tensor(dst, bank[2 * (h0 % 2)][:].rearrange("p (j c) -> p j c", j=4),
                                            masks[:, 0:1, :].broadcast_to([P, 4, P]), ALU.mult).then_inc(ba_out, 1)

                def pairs_in(t):
                    for hh in range(RH):
                        n = t * RH + hh
                        dve.wait_ge(pairs_mm, n + 1)
                        b = bank[(0, 4)[hh % 2] + hh // 2 % 2]
                        chain(nc.vector.tensor_tensor(pairs[:, hh, 0, :], b[:, 0:P], masks[:, 1, :], ALU.mult))
                        nc.vector.tensor_tensor(pairs[:, hh, 1:3, :], b[:, P:3 * P].rearrange("p (a c) -> p a c", a=2),
                                                masks[:], ALU.mult).then_inc(pairs_out, 1)

                pairs_in(0)
                chain(nc.vector.memset(inv_out[:], 0.0))
                chain(nc.vector.memset(inv_out[:].rearrange("p s u -> p (s u)")[:, 0:CH * CH:CH + 1], 1.0))
                dve.wait_ge(inv_loaded, 16)
                for s_ in range(CH - 2, -1, -1):
                    n = CH - 1 - s_
                    tmp = inv_tmp[:, 0:n * n].rearrange("p (u s) -> p u s", u=n)
                    chain(nc.vector.tensor_tensor(tmp, inv_out[:, s_ + 1:CH, s_ + 1:CH].rearrange("p s u -> p u s"),
                                                  inv_in[:, s_:s_ + 1, s_ + 1:CH].broadcast_to([P, n, n]), ALU.mult))
                    ins = nc.vector.tensor_reduce(inv_out[:, s_, s_ + 1:CH], tmp, AX.X, ALU.add)
                    if s_:
                        chain(ins)
                    else:
                        ins.then_inc(inv_made, 1)
                for t in range(TT):
                    if t:
                        pairs_in(t)
                    for cc in range(4):
                        c = 4 * t + cc
                        rows = slice(cc * CH, (cc + 1) * CH)
                        heads = lambda x: x[rows, t, :].rearrange("p (j e c) -> p j e c", e=2, c=HD)
                        if cc == 0:
                            dve.wait_ge(u0_out, 2 * t + 2)
                        for e in range(2):
                            dve.wait_ge(u_mm, 2 * c + e + 1)
                            nc.vector.tensor_tensor(heads(U)[:, :, e, :], bank[e][rows, :].rearrange("p (j c) -> p j c", c=HD),
                                                    heads(U0)[:, :, e, :], ALU.add).then_inc(u_ready, 1)
                        dve.wait_ge(s_mm, c + 1)
                        chain(nc.vector.tensor_tensor(S[:], S[:], bank[2 + c % 2][:].rearrange("p (j c) -> p j c", c=HD),
                                                      ALU.add))
                        nc.vector.tensor_tensor(S[:], S[:], chunk_decay[:, :, c:c + 1].broadcast_to([P, KD, HD]), ALU.mult
                                                ).then_inc(s_ready, 1)
                    for d in range(2):
                        ds = slice(d * HALF, (d + 1) * HALF)
                        dve.wait_ge(yg_ready, 2 * t + d + 1)
                        dve.wait_ge(ys_out, 2 * t + 2)
                        nc.vector.tensor_tensor(y_tok[:, t, ds], y_tok[:, t, ds], bank[6 + d][:], ALU.add
                                                ).then_inc(y_sum, 1)
                    dve.wait_ge(y_sum, 2 * t + 2)
                    yh = y_tok[:, t, :].rearrange("p (h c) -> p h c", c=HD)
                    mean, var = rstat[:, 64:64 + RH], rstat[:, 32:32 + RH]
                    chain(nc.vector.tensor_reduce(mean, yh, AX.X, ALU.add))
                    chain(nc.vector.tensor_scalar(mean, mean, 1.0 / HD, None, ALU.mult))
                    chain(nc.vector.tensor_tensor(yh, yh, mean.unsqueeze(2).broadcast_to([P, RH, HD]), ALU.subtract))
                    for d in range(2):
                        ds = slice(d * HALF, (d + 1) * HALF)
                        chain(nc.vector.tensor_tensor(gn_sq[:], y_tok[:, t, ds], y_tok[:, t, ds], ALU.mult))
                        chain(nc.vector.tensor_reduce(var[:, 8 * d:8 * d + 8], gn_sq[:].rearrange("p (h c) -> p h c", c=HD),
                                                      AX.X, ALU.add))
                    nc.vector.tensor_scalar(var, var, 1.0 / HD, GN_EPS, ALU.mult, ALU.add).then_inc(gn_var, 1)
                    dve.wait_ge(gn_root, t + 1)
                    rstd = rstat[:, 48:48 + RH]
                    chain(nc.vector.reciprocal(rstd, rstd))
                    chain(nc.vector.tensor_tensor(yh, yh, rstd.unsqueeze(2).broadcast_to([P, RH, HD]), ALU.mult))
                    dve.wait_ge(ln_in, 2 * 16)
                    y = y_tok[:, t, :]
                    chain(nc.vector.tensor_tensor(y, y, ln[:, 0, :], ALU.mult))
                    chain(nc.vector.tensor_tensor(y, y, ln[:, 1, :], ALU.add))
                    dve.wait_ge(bonus_out, 1)
                    vh = v_tok[:, t, :].rearrange("p (h c) -> p h c", c=HD)
                    bonus = rstat[:, t * RH:(t + 1) * RH].unsqueeze(2).broadcast_to([P, RH, HD])
                    dve.wait_ge(yg_ready, 2 * t + 2)
                    chain(nc.vector.tensor_tensor(vh, vh, bonus, ALU.mult))
                    chain(nc.vector.tensor_tensor(y, y, v_tok[:, t, :], ALU.add))
                    dve.wait_ge(g_out, 4)
                    for d in range(2):
                        ds = slice(d * HALF, (d + 1) * HALF)
                        nc.vector.tensor_tensor(y_tok[:, t, ds], y_tok[:, t, ds], g_tok[:, t, ds], ALU.mult
                                                ).then_inc(m_ready, 1)
                for i in range(2):
                    rest_in(RWKV_OUT0 + i)
                for i in range(4):
                    t, d = divmod(i, 2)
                    dve.wait_ge(m_hi, i + 1)
                    part = (slice(None), slice(4 * d, 4 * d + 4), slice(t * P, (t + 1) * P))
                    nc.vector.tensor_tensor(xT_lo[part], bank[i][:].rearrange("p (k c) -> p k c", k=4),
                                            xT_hi[part].bitcast(F32), ALU.subtract).then_inc(m_split, 1)
                for i in range(2):
                    for half in range(TT):
                        dve.wait_ge(g_ready[half], RWKV_OUT0 + i + 1)
                        cs = slice(i * HALF, (i + 1) * HALF)
                        chain(nc.vector.tensor_tensor(xn[:, half], G[half][:], mods[:, 2 * 5 + i], ALU.mult))
                        nc.vector.tensor_tensor(h[:, half, cs], h[:, half, cs], xn[:, half], ALU.add
                                                ).then_inc(h_ready, 1)

            def ffn(f, q):
                if f:
                    rest_of_block(FFN_BLOCK0[f], FFN_BLOCK0[f] % 2)
                    modulate(q, *((0, 1) if f % 2 == 0 else (6, 7)), (18, 18, 29, 36)[f])
                n0 = FFN_BLOCK0[f]
                v0, nv = ADA_FFN[f]

                def step(b, odd, ada):
                    ub, n = f * NB + b, n0 + b
                    peeled = isinstance(b, int)
                    if not (peeled and b == 0):
                        times_up(ub - 1, 1)
                        rest_of_hidden(ub - 1, 0)
                        rest_of_down(ub - 1)
                    if not (peeled and b == NB - 1):
                        rest_of_block(n + 1, (n0 + odd + 1) % 2)
                    times_up(ub, 0)
                    if not (peeled and b == 0):
                        rest_of_hidden(ub - 1, 1)
                    if ada:
                        ada_products(v0 + b)

                run_blocks(dve, f, step)
                last = f * NB + NB - 1
                times_up(last, 1)
                rest_of_hidden(last, 0)
                rest_of_down(last)
                rest_of_hidden(last, 1)
                for half in range(2):
                    dve.wait_ge(d_done[half], last + 1)
                residual(q, 2 if f % 2 == 0 else 8, 0.5, v0 + nv)

            def head_norms(srcs, heads, s0):
                for t, src in enumerate(srcs):
                    sq = squares[:, 0:heads * HD]
                    chain(nc.vector.tensor_tensor(sq, src, src, ALU.mult))
                    r = dstat[:, s0 + t * heads:s0 + (t + 1) * heads]
                    chain(nc.vector.tensor_reduce(r, sq.rearrange("p (h c) -> p h c", h=heads), AX.X, ALU.add))
                r = dstat[:, s0:s0 + len(srcs) * heads]
                nc.vector.tensor_scalar(r, r, 1.0 / HD, RMS_EPS, ALU.mult, ALU.add).then_inc(mean_ready, 1)
                count["root"] += 1
                dve.wait_ge(mean_root, count["root"])
                chain(nc.vector.reciprocal(r, r))
                return [r[:, t * heads:(t + 1) * heads].unsqueeze(2).broadcast_to([P, heads, HD])
                        for t in range(len(srcs))]

            def dsa(q):
                def rest_in(i):
                    n = DSA_BLOCK0 + i
                    rest_of_block(n, n % 2, DSA_IN[i][1] if i < len(DSA_IN) else HALF)

                def heads_of(ap):
                    return ap.rearrange("p (h c) -> p h c", c=HD)

                rest_in(0)
                modulate(q, 3, 4, 15)
                ada_products(15)
                rest_in(1)
                ada_products(16)
                rest_in(2)
                ada_products(17)
                rest_in(3)
                for t in range(TT):
                    dve.wait_ge(z_out[t], 1)
                rs = head_norms([z_small[:, t, 0:HD] for t in range(TT)], 1, 0)
                for t in range(TT):
                    chain(nc.vector.tensor_tensor(ik_twice[:, t, 0:1, :], heads_of(z_small[:, t, 0:HD]), rs[t], ALU.mult))
                    chain(nc.vector.tensor_copy(ik_twice[:, t, 1:2, :], ik_twice[:, t, 0:1, :]))
                head_w = z_small[:, :, HD:HD + IH]
                nc.vector.tensor_scalar(head_w, head_w, IH ** -0.5 * HD ** -0.5, None, ALU.mult).then_inc(small_normed, 1)
                rest_in(4)
                for t in range(TT):
                    dve.wait_ge(z_out[t], 3)
                qs = [z[:, t, 0:QH * HD] for t in range(TT)]
                rs = head_norms(qs, QH, 16)
                for t in range(TT):
                    nc.vector.tensor_tensor(heads_of(qs[t]), heads_of(qs[t]), rs[t], ALU.mult).then_inc(q_normed, 1)
                rest_in(5)
                for t in range(TT):
                    dve.wait_ge(z_out[t], 4)
                ks = [z[:, t, 2 * HALF:2 * HALF + KVH * HD] for t in range(TT)]
                rs = head_norms(ks, KVH, 4)
                for t in range(TT):
                    if t:
                        dve.wait_ge(group_turned, 6)
                    chain(nc.vector.tensor_tensor(k_twice[:, :, 0, :], heads_of(ks[t]), rs[t], ALU.mult))
                    nc.vector.tensor_copy(k_twice[:, :, 1, :], k_twice[:, :, 0, :]).then_inc(k_normed, 1)
                dve.wait_ge(small_normed, 1)

                seen = [0, 0]
                for i, (_, t, heads) in enumerate(SCORES):
                    keys = (t + 1) * P
                    dve.wait_ge(relu_ready, i + 1)
                    for j, hh in enumerate(heads):
                        part = relu[:, i % 2, j * keys:(j + 1) * keys]
                        w = z_small[:, t, HD + hh:HD + hh + 1]
                        acc_t = score[:, t, 0:keys]
                        if seen[t] == 0:
                            ins = nc.vector.tensor_scalar(acc_t, part, w, None, ALU.mult)
                        else:
                            ins = nc.vector.scalar_tensor_tensor(out=acc_t, in0=part, scalar=w, in1=acc_t,
                                                                 op0=ALU.mult, op1=ALU.add)
                        seen[t] += 1
                        if j < len(heads) - 1:
                            chain(ins)
                    ins.then_inc(relu_used, 1)
                    dve.wait_ge(relu_used, i + 1)
                rest_in(6)
                for t in range(TT):
                    keys = score[:, t, 0:(t + 1) * P]
                    dve.wait_ge(score_masked, t + 1)
                    for _ in range(TOPK // 8):
                        chain(nc.vector.max(top8[:], keys))
                        chain(nc.vector.match_replace(keys, top8[:], keys, TAKEN))
                    nc.vector.tensor_scalar(offset[:, t, 0:(t + 1) * P], keys, (NEG + TAKEN) / 2, HIDDEN, ALU.is_gt,
                                            ALU.mult).then_inc(offset_ready, 1)

                dve.wait_ge(offset_masked, TT)
                for i in range(2 * QH + 1):
                    if i < 2 * QH:
                        t = i % 2
                        keys = (t + 1) * P
                        dve.wait_ge(logits_ready, i + 1)
                        if i >= 4:
                            dve.wait_ge(probs_turned, i - 3)
                        p = probs[:, i % 4, 0:keys]
                        chain(nc.vector.tensor_tensor_reduce(p, bank[i % 4][:, 0:keys], offset[:, t, 0:keys],
                                                             HD ** -0.5, NEG, ALU.add, ALU.max,
                                                             dstat[:, 4 + i % 4:5 + i % 4]))
                        nc.vector.tensor_scalar(dstat[:, 8 + i % 4:9 + i % 4], dstat[:, 4 + i % 4:5 + i % 4], -1.0, None,
                                                ALU.mult).then_inc(max_ready, 1)
                    if i:
                        k = i - 1
                        dve.wait_ge(exp_ready, k + 1)
                        total = dstat[:, 12 + k % 4:13 + k % 4]
                        chain(nc.vector.reciprocal(total, total))
                        p = probs[:, k % 4, 0:(k % 2 + 1) * P]
                        nc.vector.tensor_scalar(p, p, total, None, ALU.mult).then_inc(probs_ready, 1)
                    if i >= 10 and i % 4 == 2:
                        heads_out((i - 10) // 4)
                for j in range(QH // 2 - 2, QH // 2):
                    heads_out(j)
                for i in range(2):
                    ks = slice(4 * i, 4 * i + 4)
                    dve.wait_ge(oT_hi_ready, i + 1)
                    nc.vector.tensor_tensor(xT_lo[:, ks, :], oT[i], xT_hi[:, ks, :].bitcast(F32), ALU.subtract
                                            ).then_inc(oT_ready, 1)
                for i in range(2):
                    for half in range(TT):
                        dve.wait_ge(g_ready[half], DSA_OUT0 + i + 1)
                        cols = slice(i * HALF, (i + 1) * HALF)
                        chain(nc.vector.tensor_tensor(xn[:, half], G[half][:], mods[:, 2 * 5 + i], ALU.mult))
                        nc.vector.tensor_tensor(h[:, half, cols], h[:, half, cols], xn[:, half], ALU.add
                                                ).then_inc(h_ready, 1)

            def heads_out(j):
                dve.wait_ge(o_ready, 2 * j + 2)
                nc.vector.tensor_copy(oT[j // 4][:, j % 4, :], bank[6 + j % 2][:, 0:SEQ]).then_inc(oT_out, 1)

            dve.wait_ge(consts, 4)
            dve.wait_ge(c_ready, 1)
            for v in range(ADA_FRONT):
                ada_products(v, v == 0)
            modulate(0, 0, 1, 4)
            rest_of_block(0, 0)
            ffn(0, 0)
            dsa(1)
            ffn(1, 2)
            ffn(2, 3)
            rwkv(4)
            ffn(3, 5)


_INS = ['x', 'c', 'ada_w', 'ada_b', 'ffn_w_gu', 'ffn_w_down', 'dsa_w_in', 'dsa_q_norm', 'dsa_k_norm', 'dsa_ik_norm',
        'dsa_w_out', 'rwkv_mu', 'rwkv_w_rkv', 'rwkv_w0', 'rwkv_w1', 'rwkv_w2', 'rwkv_a0', 'rwkv_a1', 'rwkv_a2',
        'rwkv_g1', 'rwkv_g2', 'rwkv_k_k', 'rwkv_k_a', 'rwkv_r_k', 'rwkv_ln_w', 'rwkv_ln_b', 'rwkv_w_out']
_OUT = ((1, 256, 1024), 'float32')


def kernel(**inputs):
    import numpy as _np
    import concourse.bacc as _bacc
    from concourse import mybir as _mybir
    from concourse.bass_utils import run_bass_kernel_spmd as _run

    nc = _bacc.Bacc("TRN2", target_bir_lowering=False, num_devices=1)
    arrays, args = {}, {}
    for name in _INS:
        v = _np.ascontiguousarray(inputs[name])
        arrays[f"in_{name}_dram"] = v
        args[name] = nc.dram_tensor(f"in_{name}_dram", v.shape, _mybir.dt.from_np(v.dtype), kind="ExternalInput").ap()
    out = nc.dram_tensor("out_0_dram", _OUT[0], _mybir.dt.from_np(_np.dtype(_OUT[1])), kind="ExternalOutput").ap()
    trunk(nc, args, out)
    r = _run(nc, [arrays], core_ids=[0])
    return r.results[0]["out_0_dram"]
```

```python
from contextlib import ExitStack

import concourse.bass as bass
from concourse import mybir

P = 128
F32 = mybir.dt.float32
F32R = mybir.dt.float32r
BF16 = mybir.dt.bfloat16
ALU = mybir.AluOpType
ACT = mybir.ActivationFunctionType
AX = mybir.AxisListType

RMS_EPS = 1e-6


def trunk(nc, a, out):
    SEQ, D = a["x"].shape[1:]
    TT = SEQ // P
    KD = D // P
    FF = a["ffn_w_down"].shape[2]
    FB = 256
    NB = FF // FB
    HD = 64
    QH = a["dsa_w_out"].shape[1] // HD
    KVH = 4
    IH = 8
    TOPK = min(256, SEQ // 4)
    DSA_SMALL = HD + IH
    CH = 32
    NC = SEQ // CH
    RH = a["rwkv_r_k"].shape[1]
    WA, GL = a["rwkv_w1"].shape[2], a["rwkv_g1"].shape[2]
    DECAY = 0.6065306597126334
    GN_EPS = 64e-5
    NEG = -3.0e38
    TAKEN = -3.4e38
    HIDDEN = -1.0e30
    HALF = 512
    NMOD = a["ada_w"].shape[2] // D
    HV = NMOD * D // HALF
    assert TT == 2 and KD == 8 and FF == NB * FB and NB == 11

    FFN_BLOCK0 = (0, 18, 29, 48)
    ADA_FRONT = 4
    ADA_FFN = ((4, NB), (18, NB), (29, 7), (36, 0))

    ctx = ExitStack()
    with ctx:
        ctx.enter_context(nc.allow_non_contiguous_dma(reason="columns of small vectors"))

        def sb(name, shape, dt=F32):
            return ctx.enter_context(nc.sbuf_tensor(name, shape, dt))

        def sem(name):
            return ctx.enter_context(nc.semaphore(name))

        top = {"at": -(-nc.sbuf_base // 64) * 64}

        def place(name, shape, dt=F32, at=None):
            size = 1
            for n in shape[1:]:
                size *= n
            size *= 2 if dt == BF16 else 4
            start = top["at"] if at is None else at
            t = nc.alloc_sbuf_tensor_at(name, shape, dt, offset=start)
            if at is None:
                top["at"] = -(-(start + size) // 32) * 32
            return t

        gu_hi_at = top["at"]
        gu_hi = place("gu_hi", [P, 2, KD, HALF], F32R)
        gu_lo = place("gu_lo", [P, 2, KD, HALF], F32R)
        raw_at = top["at"]
        raw = place("raw", [P, 3, 4 * HALF])
        mods_at = top["at"]
        mods = place("mods", [P, HV, HALF])
        h = place("h", [P, TT, D])
        xT_at = top["at"]
        xT_hi = place("xT_hi", [P, KD, SEQ], F32R)
        xT_lo = place("xT_lo", [P, KD, SEQ], F32R)
        ident = place("ident", [P, P])
        ones = place("ones", [P, P])
        ccol = place("ccol", [P, KD])
        cact = place("cact", [P, KD])
        stat = place("stat", [P, 16])
        masks = place("masks", [P, 2, P])
        block_ones = place("block_ones", [P, P])
        mu = place("mu", [P, 6, KD])
        cols = place("cols", [P, 6, KD])
        rk_heads = place("rk_heads", [P, KD, 2])
        chunk_decay = place("chunk_decay", [P, KD, NC])
        rstat = place("rstat", [P, 128])
        head_gain = place("head_gain", [P, 3])
        dn_at = top["at"]
        dn_hi = place("dn_hi", [P, 2, D], F32R)
        dn_lo = place("dn_lo", [P, 2, D], F32R)
        hT_at = top["at"]
        hT_hi = place("hT_hi", [P, TT, 2, P], F32R)
        hT_lo = place("hT_lo", [P, TT, 2, P], F32R)
        hid_at = top["at"]
        hid = place("hid", [P, TT, FB])
        xn_at = top["at"]
        xn = place("xn", [P, 2, HALF])
        junk_at = top["at"]
        junk = place("junk", [P, D], BF16)
        ada_at = top["at"]
        ada_raw = place("ada_raw", [P, 4, 2, HALF])
        ada_acc = place("ada_acc", [P, HALF])
        ada_bias = place("ada_bias", [P, HALF])
        spare_at = top["at"]

        z = place("z", [P, TT, 4 * HALF], at=dn_at)
        qT = place("qT", [P, QH // 2, SEQ], at=xT_at)
        kT = place("kT", [P, KVH, SEQ], at=xT_at + 8192)
        iqT = place("iqT", [P, IH // 2, SEQ], at=xT_at + 12288)
        score = place("score", [P, TT, SEQ], at=hT_at)
        offset = place("offset", [P, TT, SEQ], at=hT_at + 2048)
        relu = place("relu", [P, 2, HALF], at=xn_at)
        squares = place("squares", [P, D], at=xn_at)
        r0 = mods_at
        v_tok = place("v_tok", [P, TT, D], at=r0)
        g_tok = place("g_tok", [P, TT, D], at=r0 + 8192)
        hid_wa = place("hid_wa", [P, SEQ], at=r0 + 16384)
        hid_g = place("hid_g", [P, 2, SEQ], at=r0 + 16384 + 1024)
        K1 = 1024
        uT = place("uT", [P, KD, SEQ], at=dn_at)
        xxT = place("xxT", [P, KD, SEQ], at=dn_at + 8 * K1)
        rT = place("rT", [P, KD, SEQ], at=dn_at + 16 * K1)
        kTc = place("kTc", [P, KD, SEQ], at=dn_at + 24 * K1)
        sigT = place("sigT", [P, KD, SEQ], at=dn_at + 32 * K1)
        aT = place("aT", [P, KD, SEQ], at=dn_at + 40 * K1)
        mix = [place("mix_w", [P, KD, SEQ], at=xT_at), place("mix_a", [P, KD, SEQ], at=xT_at + 8192),
               place("mix_tmp", [P, KD, SEQ], at=dn_at + 48 * K1)]
        wa2 = place("wa2", [P, D], at=dn_at + 16 * K1)
        g2 = place("g2", [P, 2, D], at=dn_at + 20 * K1)
        w1 = place("w1", [P, KD, WA], at=ada_at)
        a1 = place("a1", [P, KD, WA], at=ada_at + 2048)
        g1 = place("g1", [P, KD, GL], at=ada_at + 4096)
        gu_at = gu_hi_at
        AR = place("AR", [P, KD, TT, 2, P], at=gu_at)
        bT = place("bT", [P, KD, SEQ], at=gu_at + 16 * K1)
        kdT = place("kdT", [P, KD, SEQ], at=gu_at + 24 * K1)
        tok = place("tok", [P, 3, TT, D], at=gu_at + 32 * K1)
        kv = place("kv", [P, NC, HALF], at=gu_at + 16 * K1)
        U = place("U", [P, TT, D], at=gu_at + 56 * K1)
        WT = place("WT", [P, KD, SEQ], at=xT_at)
        U0 = place("U0", [P, TT, D], at=xT_at + 8192)
        cum = place("cum", [P, KD, SEQ], at=dn_at)
        keep = place("keep", [P, KD * SEQ], at=dn_at + 8 * K1)
        decay_before = place("decay_before", [P, KD, SEQ], at=dn_at + 8 * K1)
        decay_in = place("decay_in", [P, KD, SEQ], at=dn_at + 48 * K1)
        gain = place("gain", [P, KD, SEQ], at=dn_at + 48 * K1)
        norm = place("norm", [P, KD, SEQ], at=dn_at + 32 * K1)
        kk = place("kk", [P, KD, SEQ], at=raw_at + 16 * K1)
        pairs = [place("pairs_0", [P, RH, 3, P], at=dn_at), place("pairs_1", [P, RH, 3, P], at=raw_at)]
        out_raw = place("out_raw", [P, 2, 4 * HALF], at=dn_at)
        inv = place("inv", [P, TT, RH, P], at=dn_at + 24 * K1)
        inv_in = place("inv_in", [P, CH, CH], at=dn_at + 40 * K1)
        inv_out = place("inv_out", [P, CH, CH], at=dn_at + 44 * K1)
        inv_tmp = place("inv_tmp", [P, CH * CH], at=dn_at + 48 * K1)
        y_tok = place("y_tok", [P, TT, D], at=dn_at + 40 * K1)
        ln = place("ln", [P, 2, D], at=dn_at + 48 * K1)
        S = place("S", [P, KD, HD], at=r0 + 16384)
        gn_sq = place("gn_sq", [P, HALF], at=r0 + 16384 + 2048)
        z_small = place("z_small", [P, TT, DSA_SMALL], at=spare_at)
        k_twice = place("k_twice", [P, KVH, 2, HD], at=junk_at)
        ik_twice = place("ik_twice", [P, TT, 2, HD], at=hid_at)
        ikT = place("ikT", [P, SEQ], at=hid_at + 1024)
        probs = place("probs", [P, 4, SEQ], at=spare_at + 640)
        probsT = place("probsT", [P, 2, 3 * P], at=spare_at + 640 + 4096)
        dstat = place("dstat", [P, 64], at=spare_at + 640 + 4096 + 3072)
        top8 = place("top8", [P, 8], at=spare_at + 640 + 4096 + 3072 + 256)
        oT = [z[:, i, 0:D].rearrange("p (j c) -> p j c", j=QH // 4) for i in range(TT)]

        bank = [ctx.enter_context(nc.psum_tensor(f"bank{i}", [P, HALF], F32)) for i in range(8)]
        acc = [[bank[0], bank[1]], [bank[2], bank[3]]]
        G = [bank[4], bank[5]]
        TB = [bank[6], bank[7]]

        consts = sem("consts")
        c_in = sem("c_in")
        h_in = sem("h_in")
        c_ready = sem("c_ready")
        raw_in = [sem("raw_in_a"), sem("raw_in_b"), sem("raw_in_down")]
        hi_ready = [sem("hi_a"), sem("hi_b"), sem("hi_down")]
        split = [sem("split_a"), sem("split_b"), sem("split_down")]
        ada_in = [sem(f"ada_in_{i}") for i in range(4)]
        bias_in = sem("bias_in")
        ada_step = sem("ada_step")
        ada_sum = sem("ada_sum")
        mods_ready = sem("mods_ready")
        g_ready = [sem("g_ready_0"), sem("g_ready_1")]
        silu_done = [sem("silu_0"), sem("silu_1")]
        hid_ready = [sem("hid_ready_0"), sem("hid_ready_1")]
        t_ready = [sem("t_ready_0"), sem("t_ready_1")]
        hT_hi_ready = [sem("hT_hi_0"), sem("hT_hi_1")]
        hT_ready = [sem("hT_ready_0"), sem("hT_ready_1")]
        d_done = [sem("d_done_0"), sem("d_done_1")]
        dve_step = sem("dve_step")
        h_ready = sem("h_ready")
        square_sum = sem("square_sum")
        root = sem("root")
        rstd_var = sem("rstd_var")
        xn_ready = sem("xn_ready")
        xn_turned = sem("xn_turned")
        xT_hi_ready = sem("xT_hi_ready")
        xT_ready = sem("xT_ready")
        stored = sem("stored")
        gains_in = sem("gains_in")
        z_out = [sem("z_out_0"), sem("z_out_1")]
        small_normed = sem("small_normed")
        q_normed = sem("q_normed")
        k_normed = sem("k_normed")
        mean_ready = sem("mean_ready")
        mean_root = sem("mean_root")
        group_turned = sem("group_turned")
        group_out = sem("group_out")
        scores_ready = sem("scores_ready")
        relu_ready = sem("relu_ready")
        relu_used = sem("relu_used")
        score_masked = sem("score_masked")
        offset_ready = sem("offset_ready")
        offset_masked = sem("offset_masked")
        logits_ready = sem("logits_ready")
        max_ready = sem("max_ready")
        exp_ready = sem("exp_ready")
        probs_ready = sem("probs_ready")
        probs_turned = sem("probs_turned")
        probsT_ready = sem("probsT_ready")
        o_ready = sem("o_ready")
        oT_out = sem("oT_out")
        oT_hi_ready = sem("oT_hi_ready")
        oT_ready = sem("oT_ready")
        rwkv_in = sem("rwkv_in")
        lora1_in = sem("lora1_in")
        lora2_in = sem("lora2_in")
        uT_ready = sem("uT_ready")
        mix_ready = sem("mix_ready")
        reads_ready = sem("reads_ready")
        gain_ready = sem("gain_ready")
        kd_ready = sem("kd_ready")
        rstd_ready = sem("rstd_ready")
        kt_ready = sem("kt_ready")
        mix_hi_ready = sem("mix_hi_ready")
        mix_split = sem("mix_split")
        lora_ready = sem("lora_ready")
        wa_hid_ready = sem("wa_hid_ready")
        wa_ready = sem("wa_ready")
        g_out = sem("g_out")
        wa_out = sem("wa_out")
        v_out = sem("v_out")
        rc_out = sem("rc_out")
        kk_sum = sem("kk_sum")
        kk_root = sem("kk_root")
        cum_ready = sem("cum_ready")
        decay_out = sem("decay_out")
        ops_ready = sem("ops_ready")
        rk_ready = sem("rk_ready")
        bonus_ready = sem("bonus_ready")
        bonus_out = sem("bonus_out")
        tok_turned = sem("tok_turned")
        tok_out = sem("tok_out")
        ba_ready = sem("ba_ready")
        ba_out = sem("ba_out")
        inv_saved = sem("inv_saved")
        inv_loaded = sem("inv_loaded")
        inv_made = sem("inv_made")
        inv_stored = sem("inv_stored")
        inv_back = sem("inv_back")
        pairs_mm = sem("pairs_mm")
        pairs_out = sem("pairs_out")
        x1_ready = sem("x1_ready")
        x1_out = sem("x1_out")
        u0_ready = sem("u0_ready")
        u0_out = sem("u0_out")
        wt_ready = sem("wt_ready")
        wt_out = sem("wt_out")
        u_mm = sem("u_mm")
        u_ready = sem("u_ready")
        s_mm = sem("s_mm")
        s_ready = sem("s_ready")
        ys_ready = sem("ys_ready")
        ys_out = sem("ys_out")
        yg_ready = sem("yg_ready")
        y_sum = sem("y_sum")
        gn_var = sem("gn_var")
        gn_root = sem("gn_root")
        m_ready_0 = sem("m_ready_0")
        m_ready_1 = sem("m_ready_1")
        m_turned = sem("m_turned")
        m_hi = sem("m_hi")
        m_split = sem("m_split")
        ln_in = sem("ln_in")
        zeroed = sem("zeroed")
        masks_made = sem("masks_made")
        gn_step = sem("gn_step")
        pairs_raw = sem("pairs_raw")
        kv_mm = sem("kv_mm")
        kv_out = sem("kv_out")
        m_ready = [m_ready_0, m_ready_1]

        ffn_gu = a["ffn_w_gu"].rearrange("l j (k p) (g c) -> l j p k g c", p=P, g=2)
        ffn_dn = a["ffn_w_down"].rearrange("l j (t p) d -> l j p t d", p=P)
        ada_w = a["ada_w"].rearrange("l (k p) n -> l p k n", p=P)

        DSA_BLOCK0, DSA_OUT0 = 11, 16
        DSA_IN = [(2048, DSA_SMALL, lambda t: z_small[:, t, :]), (0, HALF, lambda t: z[:, t, 0:HALF]),
                  (HALF, HALF, lambda t: z[:, t, HALF:2 * HALF]), (2 * HALF, HALF, lambda t: z[:, t, 2 * HALF:3 * HALF]),
                  (3 * HALF, HALF, lambda t: z[:, t, 3 * HALF:4 * HALF])]
        GROUPS = [(0, "ik", None, 0), (1, "iq", 0, 0), (2, "iq", 1, 0), (3, "q", 0, 0), (6, "q", 0, 4), (7, "k", 0, 0),
                  (0, "k", 1, 0), (1, "q", 1, 0), (2, "q", 1, 4)]
        SCORES = [(4, 0, (0, 2, 4, 6)), (5, 0, (1, 3, 5, 7)), (3, 1, (0, 2)), (6, 1, (4, 6)), (7, 1, (1, 3)), (0, 1, (5, 7))]
        V0 = 2 * HALF + KVH * HD

        V_BLOCK, R_BLOCK, K_BLOCK, RWKV_OUT0 = 40, 42, 44, 46
        inv_dram = [nc.dram_tensor(f"inverse_{i}", [TT * 4 * RH, CH * CH], F32, kind="Internal").ap() for i in range(2)]

        g_ready_rwkv = sem("g_ready_rwkv")

        def blocks_of(f):
            n = ADA_FFN[f][1]
            if n in (0, NB):
                return [(0, 3, False), (3, 6, True), (9, 2, False)]
            return [(0, 3, False), (3, 4, True), (7, 4, False)]

        def run_blocks(eng, f, step):
            for first, count, loop in blocks_of(f):
                nv = ADA_FFN[f][1]
                if not loop:
                    for b in range(first, first + count):
                        step(b, b % 2, b < nv)
                else:
                    with eng.Fori(first, first + count - 1, 2) as b:
                        step(b, first % 2, first < nv)
                        step(b + 1, (first + 1) % 2, first < nv)

        def group_norm(eng, t, chained):
            yh = y_tok[:, t, :].rearrange("p (h c) -> p h c", c=HD)
            var, mean = rstat[:, 32 + t * RH:32 + (t + 1) * RH], rstat[:, 96 + t * RH:96 + (t + 1) * RH]
            chained(eng.tensor_reduce(mean, yh, AX.X, ALU.add))
            chained(eng.tensor_scalar(mean, mean, 1.0 / HD, None, ALU.mult))
            chained(eng.tensor_tensor(yh, yh, mean.unsqueeze(2).broadcast_to([P, RH, HD]), ALU.subtract))
            for d in range(2):
                ds = slice(d * HALF, (d + 1) * HALF)
                chained(eng.tensor_tensor(gn_sq[:], y_tok[:, t, ds], y_tok[:, t, ds], ALU.mult))
                chained(eng.tensor_reduce(var[:, 8 * d:8 * d + 8], gn_sq[:].rearrange("p (h c) -> p h c", c=HD),
                                          AX.X, ALU.add))
            return eng.tensor_scalar(var, var, 1.0 / HD, GN_EPS, ALU.mult, ALU.add)

        def group_scale(eng, t, chained):
            yh = y_tok[:, t, :].rearrange("p (h c) -> p h c", c=HD)
            y, rstd = y_tok[:, t, :], rstat[:, 64 + t * RH:64 + (t + 1) * RH]
            chained(eng.tensor_tensor(yh, yh, rstd.unsqueeze(2).broadcast_to([P, RH, HD]), ALU.mult))
            chained(eng.tensor_tensor(y, y, ln[:, 0, :], ALU.mult))
            chained(eng.tensor_tensor(y, y, ln[:, 1, :], ALU.add))
            vh = v_tok[:, t, :].rearrange("p (h c) -> p h c", c=HD)
            bonus = rstat[:, t * RH:(t + 1) * RH].unsqueeze(2).broadcast_to([P, RH, HD])
            chained(eng.tensor_tensor(vh, vh, bonus, ALU.mult))
            chained(eng.tensor_tensor(y, y, v_tok[:, t, :], ALU.add))
            for d in range(2):
                ds = slice(d * HALF, (d + 1) * HALF)
                eng.tensor_tensor(y_tok[:, t, ds], y_tok[:, t, ds], g_tok[:, t, ds], ALU.mult).then_inc(m_ready[t], 1)

        block = ctx.enter_context(nc.Block())

        @block.sync
        def _(sp):
            x = a["x"].rearrange("b (t p) d -> p (b t) d", p=P)
            sp.dma_start(ccol[:], a["c"].rearrange("b (k p) -> p (b k)", p=P)).then_inc(c_in, 16)
            sp.wait_ge(ada_in[3], 16 * (ADA_FRONT - 1))
            sp.dma_start(h[:], x).then_inc(h_in, 16)

            def slot_free(n, i, first):
                if not first:
                    sp.wait_ge(split[i], n)

            def load_block(n, i, left, right, first=False):
                slot_free(n, i, first)
                dst = raw[:, i, :].rearrange("p (k g c) -> p k g c", k=4, g=2)
                sp.dma_start(dst[:, :, 0, :], left).then_inc(raw_in[i], 16)
                sp.dma_start(dst[:, :, 1, :], right).then_inc(raw_in[i], 16)

            def load_mixer_block(n, w, cols, buf=raw, free=False):
                width = cols.stop - cols.start
                for i in range(2):
                    slot_free(n, i, free)
                    dst = buf[:, i, 0:4 * width].rearrange("p (k c) -> p k c", k=4)
                    src = w.rearrange("(k p) c -> p k c", p=P)
                    for j in range(2):
                        sp.dma_start(dst[:, 2 * j:2 * j + 2, :], src[:, 4 * i + 2 * j:4 * i + 2 * j + 2, cols]
                                     ).then_inc(raw_in[i], 16)

            def dsa():
                for i, name in enumerate(("dsa_q_norm", "dsa_k_norm", "dsa_ik_norm")):
                    for e in range(2):
                        sp.dma_start(head_gain[e * HD:(e + 1) * HD, i:i + 1], a[name].rearrange("l c -> c l")
                                     ).then_inc(gains_in, 16)
                for i, (c0, width, _) in enumerate(DSA_IN):
                    load_mixer_block(DSA_BLOCK0 + i, a["dsa_w_in"][0], slice(c0, c0 + width))
                for i in range(2):
                    load_mixer_block(DSA_OUT0 + i, a["dsa_w_out"][0], slice(i * HALF, (i + 1) * HALF))

            def ffn(f):
                layer, j = divmod(f, 2)
                n0 = FFN_BLOCK0[f]

                def gate_up(b, n):
                    for i in range(2):
                        rows = ffn_gu[layer, j, :, 4 * i:4 * i + 4, :, bass.ds(b * FB, FB)]
                        load_block(n, i, rows[:, :, 0, :], rows[:, :, 1, :], isinstance(n, int) and n == 0)

                def step(b, odd, ada):
                    if isinstance(b, int) and b == 0:
                        gate_up(0, n0)
                    if isinstance(b, int) and f == 0 and b == 0:
                        sp.wait_ge(ada_in[3], 16 * ADA_FRONT)
                    if not (isinstance(b, int) and b == NB - 1):
                        gate_up(b + 1, n0 + b + 1)
                    slot_free(f * NB + b, 2, isinstance(b, int) and f * NB + b == 0)
                    sp.dma_start(raw[:, 2, :].rearrange("p (t d) -> p t d", t=2),
                                 ffn_dn[layer, j, :, bass.ds(b * 2, 2), :]).then_inc(raw_in[2], 16)
                run_blocks(sp, f, step)

            def rwkv(q):
                for i in range(6):
                    sp.dma_start(mu[:, i, :], a["rwkv_mu"][0, i:i + 1, :].rearrange("o (k p) -> p (o k)", p=P)
                                 ).then_inc(rwkv_in, 16)
                for i, name in enumerate(("rwkv_w0", "rwkv_a0", "rwkv_k_k", "rwkv_k_a")):
                    sp.dma_start(cols[:, i, :], a[name].rearrange("o (k p) -> p (o k)", p=P)).then_inc(rwkv_in, 16)
                r_k = a["rwkv_r_k"].rearrange("o (k e) c -> (o e c) k", e=2)
                sp.dma_start(cols[:, 4, :], r_k).then_inc(rwkv_in, 16)
                sp.wait_ge(ada_step, 36 * KD)
                for name, dst in (("rwkv_w1", w1), ("rwkv_a1", a1), ("rwkv_g1", g1)):
                    sp.dma_start(dst[:], a[name][0].rearrange("(k p) n -> p k n", p=P)).then_inc(lora1_in, 16)
                load_mixer_block(V_BLOCK, a["rwkv_w_rkv"][0, 2], slice(0, HALF))
                sp.wait_ge(uT_ready, 4)
                sp.dma_start(wa2[0:WA, :], a["rwkv_w2"][0]).then_inc(lora2_in, 16)
                sp.dma_start(wa2[WA:2 * WA, :], a["rwkv_a2"][0]).then_inc(lora2_in, 16)
                sp.dma_start(g2[:, 0, :], a["rwkv_g2"][0, 0:P, :]).then_inc(lora2_in, 16)
                sp.dma_start(g2[0:GL - P, 1, :], a["rwkv_g2"][0, P:GL, :]).then_inc(lora2_in, 16)
                load_mixer_block(V_BLOCK + 1, a["rwkv_w_rkv"][0, 2], slice(HALF, D))
                for j in range(2):
                    for i in range(2):
                        load_mixer_block(R_BLOCK + 2 * j + i, a["rwkv_w_rkv"][0, j], slice(i * HALF, (i + 1) * HALF))
                blocks = [(t, c) for t in range(TT) for c in range(4)]

                def dram_block(i, t, c):
                    rows = slice((4 * t + c) * RH, (4 * t + c + 1) * RH)
                    return inv_dram[i][rows, :].rearrange("h (s u) -> s h u", s=CH)

                def sbuf_block(t, c):
                    return inv[c * CH:(c + 1) * CH, t, :, c * CH:(c + 1) * CH]
                sp.wait_ge(ba_out, 8)
                for t, c in blocks:
                    sp.dma_start(dram_block(0, t, c), sbuf_block(t, c)).then_inc(inv_saved, 16)
                sp.wait_ge(inv_saved, 16 * len(blocks))
                sp.wait_ge(tok_out, 12)
                sp.dma_start(inv_in[:].rearrange("p s u -> p (s u)"), inv_dram[0]).then_inc(inv_loaded, 16)
                sp.wait_ge(inv_made, 1)
                sp.dma_start(inv_dram[1], inv_out[:].rearrange("p s u -> p (s u)")).then_inc(inv_stored, 16)
                sp.wait_ge(inv_stored, 16)
                for t, c in blocks:
                    sp.dma_start(sbuf_block(t, c), dram_block(1, t, c)).then_inc(inv_back, 16)
                for i, name in enumerate(("rwkv_ln_w", "rwkv_ln_b")):
                    sp.dma_start(ln[:, i, :], a[name].broadcast_to([P, D])).then_inc(ln_in, 16)
                sp.wait_ge(yg_ready, 2)
                load_mixer_block(RWKV_OUT0, a["rwkv_w_out"][0], slice(0, HALF), out_raw)
                sp.wait_ge(yg_ready, 4)
                for i in range(2):
                    sp.wait_ge(raw_in[i], 32 * RWKV_OUT0 + 32)
                load_mixer_block(RWKV_OUT0 + 1, a["rwkv_w_out"][0], slice(HALF, D), free=True)

            ffn(0)
            dsa()
            ffn(1)
            ffn(2)
            rwkv(4)
            ffn(3)
            sp.wait_ge(h_ready, 4 * 6)
            sp.dma_start(out.rearrange("b (t p) d -> p (b t) d", p=P), h[:]).then_inc(stored, 16)
            sp.wait_ge(stored, 16)

        @block.gpsimd
        def _(pool):
            nc.gpsimd.memset(ident[:], 0.0).then_inc(consts, 1)
            nc.gpsimd.memset(ones[:], 1.0).then_inc(consts, 1)
            nc.gpsimd.memset(ada_bias[:], 0.0).then_inc(consts, 1)
            pool.wait_ge(consts, 3)
            nc.gpsimd.affine_select(out=ident[:], in_=ident[:], compare_op=ALU.not_equal, fill=1.0, base=0,
                                    pattern=[[-1, P]], channel_multiplier=1).then_inc(consts, 1)

            def causal(made, counts, buf, fill, masked):
                for t in range(TT):
                    pool.wait_ge(made, counts[t])
                    own = buf[:, t, t * P:(t + 1) * P]
                    nc.gpsimd.affine_select(out=own, in_=own, compare_op=ALU.is_ge, fill=fill, base=0,
                                            pattern=[[-1, P]], channel_multiplier=1).then_inc(masked, 1)

            nc.gpsimd.memset(masks[:], 1.0).then_inc(masks_made, 1)
            nc.gpsimd.memset(block_ones[:], 1.0).then_inc(masks_made, 1)
            made = {"masks": 2}

            def select(view, base, pattern, multiplier):
                pool.wait_ge(masks_made, made["masks"])
                nc.gpsimd.affine_select(out=view, in_=view, compare_op=ALU.is_ge, fill=0.0, base=base, pattern=pattern,
                                        channel_multiplier=multiplier).then_inc(masks_made, 1)
                made["masks"] += 1

            for i in range(2):
                view = masks[:, i, :].rearrange("p (c u) -> p c u", u=CH)
                select(view, 0, [[-CH, 4], [0, CH]], 1)
                select(view, CH - 1, [[CH, 4], [0, CH]], -1)
                select(view, i - 1, [[CH, 4], [1, CH]], -1)
            view = block_ones[:].rearrange("p (e c) -> p e c", e=2)
            select(view, 0, [[-HD, 2], [0, HD]], 1)
            select(view, HD - 1, [[HD, 2], [0, HD]], -1)

            causal(relu_used, (2, 6), score, NEG, score_masked)
            causal(offset_ready, (1, 2), offset, HIDDEN, offset_masked)

            pool.wait_ge(reads_ready, 1)
            pool.wait_ge(wa_out, 2 * KD)
            for k in range(KD):
                ins = nc.gpsimd.tensor_scalar(gain[:, k, :], aT[:, k, :], cols[:, 3, k:k + 1], cols[:, 5, k:k + 1],
                                              ALU.mult, ALU.add)
            ins.then_inc(gain_ready, 1)
            pool.wait_ge(gain_ready, 1)
            for half in range(2):
                ks = slice(4 * half, 4 * half + 4)
                pool.wait_ge(rc_out, 6 + 2 * half)
                nc.gpsimd.tensor_tensor(kTc[:, ks, :], kTc[:, ks, :], gain[:, ks, :], ALU.mult).then_inc(kt_ready, 1)
                pool.wait_ge(kt_ready, half + 1)
                nc.gpsimd.tensor_tensor(gain[:, ks, :], rT[:, ks, :], kTc[:, ks, :], ALU.mult).then_inc(rk_ready, 1)
            pool.wait_ge(decay_out, 3)
            pool.wait_ge(g_ready[1], RWKV_OUT0)
            nc.gpsimd.tensor_tensor(kdT[:], kTc[:], cum[:], ALU.mult).then_inc(kd_ready, 1)

            for g in range(TT * RH // 4):
                t, h0 = divmod(4 * g, RH)
                pool.wait_ge(pairs_raw, 4 * g + 4)
                for i in range(3):
                    view = pairs[t][:, h0:h0 + 4, i, :]
                    mask = masks[:, i % 2 ^ 1, :].unsqueeze(1).broadcast_to([P, 4, P])
                    ins = nc.gpsimd.tensor_tensor(view, view, mask, ALU.mult)
                ins.then_inc(pairs_out, 1)

            steps = {"gn": 0}

            def chained(ins):
                steps["gn"] += 1
                ins.then_inc(gn_step, 1)
                pool.wait_ge(gn_step, steps["gn"])

            pool.wait_ge(rstd_ready, 1)
            pool.wait_ge(ln_in, 2 * 16)
            pool.wait_ge(bonus_out, 1)
            pool.wait_ge(g_out, 4)
            group_scale(nc.gpsimd, 0, chained)

        @block.tensor
        def _(pe):
            def ada_total(v, spread):
                pe.wait_ge(ada_step, v * KD + KD)
                nc.tensor.matmul(spread[:], ones[:], ada_acc[:], start=True, stop=True).then_inc(ada_sum, 1)

            def turn_x(q):
                for i in range(4):
                    pe.wait_ge(xn_ready, 4 * q + i + 1)
                    for k in range(4):
                        mm = nc.tensor.transpose(bank[4 + i][:, k * P:(k + 1) * P], xn[:, i % 2, k * P:(k + 1) * P],
                                                 ident[:])
                    mm.then_inc(xn_turned, 1)

            def products(out_ap, sta_hi, sta_lo, mov_hi, mov_lo, start, stop):
                nc.tensor.matmul(out_ap, sta_hi, mov_hi, start=start, stop=False, skip_group_check=True)
                nc.tensor.matmul(out_ap, sta_hi, mov_lo, start=False, stop=False, skip_group_check=True)
                return nc.tensor.matmul(out_ap, sta_lo, mov_hi, start=False, stop=stop, skip_group_check=True)

            def gate_up(n, par, half, width=HALF):
                tok = slice(half * P, (half + 1) * P)
                for k in range(KD):
                    if half == 0 and k % 4 == 0:
                        pe.wait_ge(split[k // 4], n + 1)
                    mm = products(G[half][:, 0:width], xT_hi[:, k, tok], xT_lo[:, k, tok],
                                  gu_hi[:, par, k, 0:width], gu_lo[:, par, k, 0:width], k == 0, k == KD - 1)
                mm.then_inc(g_ready[half], 1)

            def turn_hidden(ub, half, first=False):
                pe.wait_ge(hid_ready[half], ub + 1)
                if not first:
                    pe.wait_ge(hT_ready[half], ub)
                for t in range(2):
                    mm = nc.tensor.transpose(TB[half][:, t * P:(t + 1) * P], hid[:, half, t * P:(t + 1) * P], ident[:])
                mm.then_inc(t_ready[half], 1)

            def down(ub, half, start, stop):
                pe.wait_ge(hT_ready[half], ub + 1)
                if half == 0:
                    pe.wait_ge(split[2], ub + 1)
                for t in range(2):
                    for d in range(2):
                        cols = slice(d * HALF, (d + 1) * HALF)
                        mm = products(acc[half][d][:], hT_hi[:, half, t, :], hT_lo[:, half, t, :],
                                      dn_hi[:, t, cols], dn_lo[:, t, cols], start and t == 0, stop and t == 1)
                mm.then_inc(d_done[half], 1)

            def ffn(f, q):
                turn_x(q)
                turned = 4 * (q if q < 4 else q - 1)
                pe.wait_ge(xT_ready, turned + 2)
                n0 = FFN_BLOCK0[f]
                v0, nv = ADA_FFN[f]

                def step(b, odd, ada):
                    ub, par = f * NB + b, (n0 + odd) % 2
                    peeled = isinstance(b, int)
                    if not (peeled and b == 0):
                        pe.wait_ge(hid_ready[0], ub)
                    gate_up(n0 + b, par, 0)
                    if not (peeled and b == 0):
                        turn_hidden(ub - 1, 1, peeled and ub == 1)
                        if nv and not (peeled and b > nv):
                            pe.wait_ge(hT_ready[0], ub)
                            ada_total(v0 + b - 1, TB[0])
                        down(ub - 1, 0, peeled and b == 1, False)
                        pe.wait_ge(hid_ready[1], ub)
                    else:
                        pe.wait_ge(xT_ready, turned + 4)
                    gate_up(n0 + b, par, 1)
                    if nv and not (peeled and (b == 0 or b > nv)):
                        pe.wait_ge(mods_ready, v0 + b)
                    turn_hidden(ub, 0, peeled and ub == 0)
                    if not (peeled and b == 0):
                        down(ub - 1, 1, peeled and b == 1, False)

                run_blocks(pe, f, step)
                last = f * NB + NB - 1
                turn_hidden(last, 1)
                down(last, 0, False, True)
                down(last, 1, False, True)
                if nv == NB:
                    ada_total(v0 + NB - 1, TB[0])

            def dsa(q):
                turn_x(q)
                for i, (_, width, _) in enumerate(DSA_IN):
                    n = DSA_BLOCK0 + i
                    for half in range(TT):
                        if i == 0:
                            pe.wait_ge(xT_ready, 4 * q + 2 * half + 2)
                        if i:
                            pe.wait_ge(z_out[half], i)
                        gate_up(n, n % 2, half, width)
                    if i in (1, 2, 3):
                        ada_total(14 + i, TB[i % 2])

                def turn_group(g):
                    b, what, t, first = GROUPS[g]
                    if what == "ik":
                        pe.wait_ge(small_normed, 1)
                        tiles = [ik_twice[:, t2].rearrange("p a c -> p (a c)") for t2 in range(TT)]
                    elif what == "k":
                        pe.wait_ge(k_normed, t + 1)
                        tiles = [k_twice[:, g2].rearrange("p a c -> p (a c)") for g2 in range(KVH)]
                    else:
                        if what == "q":
                            pe.wait_ge(q_normed, t + 1)
                        else:
                            pe.wait_ge(z_out[t], 5)
                        c0 = 0 if what == "q" else 3 * HALF
                        tiles = [z[:, t, c0 + (first + j) * P:c0 + (first + j + 1) * P] for j in range(4)]
                    if b >= 6:
                        pe.wait_ge(mods_ready, 18)
                    if g >= 6:
                        pe.wait_ge(group_out, g - 5)
                    for j, tile in enumerate(tiles):
                        mm = nc.tensor.transpose(bank[b][:, j * P:(j + 1) * P], tile, ident[:])
                    mm.then_inc(group_turned, 1)

                for g in range(len(GROUPS)):
                    turn_group(g)
                pe.wait_ge(group_out, len(GROUPS))
                for b, t, heads in SCORES:
                    keys = (t + 1) * P
                    pe.wait_ge(z_out[b - 4 if b in (4, 5) else 0], 5)
                    for j, hh in enumerate(heads):
                        rows = slice(hh % 2 * HD, hh % 2 * HD + HD)
                        mm = nc.tensor.matmul(bank[b][:, j * keys:(j + 1) * keys], iqT[rows, hh // 2, t * P:(t + 1) * P],
                                              ikT[rows, 0:keys], start=True, stop=True)
                    mm.then_inc(scores_ready, 1)

                pe.wait_ge(relu_ready, len(SCORES))
                for i in range(2 * QH + 6):
                    if i < 2 * QH:
                        hh, t = divmod(i, 2)
                        rows = slice(hh % 2 * HD, hh % 2 * HD + HD)
                        if i >= 4:
                            pe.wait_ge(max_ready, i - 3)
                        nc.tensor.matmul(bank[i % 4][:, 0:(t + 1) * P], qT[rows, hh // 2, t * P:(t + 1) * P],
                                         kT[rows, hh // (QH // KVH), 0:(t + 1) * P], start=True, stop=True
                                         ).then_inc(logits_ready, 1)
                    j = i - 3
                    if 0 <= j < 2 * QH:
                        hh, t = divmod(j, 2)
                        pe.wait_ge(probs_ready, j + 1)
                        if t == 0 and hh >= 2:
                            pe.wait_ge(probsT_ready, hh - 1)
                        for s in range(t + 1):
                            mm = nc.tensor.transpose(bank[4 + hh % 2][:, (t + s) * P:(t + s + 1) * P],
                                                     probs[:, j % 4, s * P:(s + 1) * P], ident[:])
                        mm.then_inc(probs_turned, 1)
                    if i >= 6 and i % 2 == 0:
                        attend((i - 6) // 2)

                pe.wait_ge(oT_ready, 2)
                for i in range(2):
                    n = DSA_OUT0 + i
                    for half in range(TT):
                        if i:
                            pe.wait_ge(h_ready, 4 * q + half + 1)
                        gate_up(n, n % 2, half)

            def attend(hh):
                j, e = divmod(hh, 2)
                pe.wait_ge(probsT_ready, hh + 1)
                if e == 0 and j >= 2:
                    pe.wait_ge(oT_out, j - 1)
                v0 = V0 + hh // (QH // KVH) * HD
                out_rows = bank[6 + j % 2][e * HD:(e + 1) * HD, :]
                nc.tensor.matmul(out_rows[:, 0:SEQ], z[:, 0, v0:v0 + HD], probsT[:, hh % 2, 0:SEQ],
                                 start=True, stop=False, skip_group_check=True)
                nc.tensor.matmul(out_rows[:, P:SEQ], z[:, 1, v0:v0 + HD], probsT[:, hh % 2, SEQ:SEQ + P],
                                 start=False, stop=True, skip_group_check=True).then_inc(o_ready, 1)

            def rwkv(q):
                turn_x(q)
                pe.wait_ge(lora1_in, 3 * 16)
                pe.wait_ge(uT_ready, 4)
                for i, (w, out_ap) in enumerate(((w1, bank[0][0:WA, 0:SEQ]), (a1, bank[1][P - WA:P, 0:SEQ]))):
                    pe.wait_ge(mix_ready, i + 1)
                    for k in range(KD):
                        mm = nc.tensor.matmul(out_ap, w[:, k, :], mix[i][:, k, :], start=k == 0, stop=k == KD - 1)
                    mm.then_inc(lora_ready, 1)
                pe.wait_ge(mix_ready, 3)
                for i, (c0, c1) in enumerate(((0, P), (P, GL))):
                    for k in range(KD):
                        mm = nc.tensor.matmul(bank[2 + i][0:c1 - c0, 0:SEQ], g1[:, k, c0:c1], mix[2][:, k, :],
                                              start=k == 0, stop=k == KD - 1)
                    mm.then_inc(lora_ready, 1)
                pe.wait_ge(lora2_in, 4 * 16)
                pe.wait_ge(wa_hid_ready, 4)
                for m in range(KD):
                    for e in range(2):
                        rows = slice(e * WA, (e + 1) * WA)
                        mm = nc.tensor.matmul(bank[4 * e + m // 2][:, m % 2 * SEQ:(m % 2 + 1) * SEQ],
                                              wa2[rows, m * P:(m + 1) * P], hid_wa[rows, :], start=True, stop=True)
                    mm.then_inc(wa_ready, 1)
                pe.wait_ge(wa_out, 2 * KD)
                for t in range(TT):
                    ts = slice(t * P, (t + 1) * P)
                    for d in range(2):
                        ds = slice(d * HALF, (d + 1) * HALF)
                        nc.tensor.matmul(acc[t][d][:], hid_g[:, 0, ts], g2[:, 0, ds], start=True, stop=False)
                        mm = nc.tensor.matmul(acc[t][d][:], hid_g[0:GL - P, 1, ts], g2[0:GL - P, 1, ds],
                                              start=False, stop=True)
                        mm.then_inc(g_ready_rwkv, 1)
                pe.wait_ge(mix_split, 1)
                for i in range(2):
                    n = V_BLOCK + i
                    for half in range(TT):
                        if i:
                            pe.wait_ge(v_out, half + 1)
                        gate_up(n, n % 2, half)
                for i in range(4):
                    n = R_BLOCK + i
                    pe.wait_ge(mix_split, 2 + i // 2)
                    for half in range(2):
                        if i:
                            pe.wait_ge(rc_out, 2 * i + half - 1)
                        else:
                            pe.wait_ge(v_out, 3 + half)
                        if half == 0:
                            for k in range(2):
                                pe.wait_ge(split[k], n + 1)
                        for m in range(2 * half, 2 * half + 2):
                            ms = slice(m * P, (m + 1) * P)
                            for k in range(KD):
                                mm = products(G[half][:, m % 2 * SEQ:(m % 2 + 1) * SEQ], gu_hi[:, n % 2, k, ms],
                                              gu_lo[:, n % 2, k, ms], xT_hi[:, k, :], xT_lo[:, k, :],
                                              k == 0, k == KD - 1)
                        mm.then_inc(g_ready[half], 1)
                        if i == 3:
                            pe.wait_ge(masks_made, 10)
                            for j in range(2 * half, 2 * half + 2):
                                pe.wait_ge(rc_out, 5 + j)
                                nc.tensor.matmul(bank[j][:], block_ones[:],
                                                 norm[:, 2 * j:2 * j + 2, :].rearrange("p k c -> p (k c)"),
                                                 start=True, stop=True).then_inc(kk_sum, 1)
                pe.wait_ge(rk_ready, 2)
                for t in range(TT):
                    for k in range(KD):
                        mm = nc.tensor.matmul(bank[4][:, t * RH + 2 * k:t * RH + 2 * k + 2],
                                              gain[:, k, t * P:(t + 1) * P], rk_heads[:, k, :], start=True, stop=True)
                mm.then_inc(bonus_ready, 1)
                pe.wait_ge(ops_ready, 1)
                for i in range(8):
                    t, h0 = divmod(i, 4)
                    b = 2 * (h0 % 2)
                    if i >= 2:
                        pe.wait_ge(ba_out, i - 1)
                    for j in range(4):
                        hh = 8 * (h0 // 2) + 2 * j + h0 % 2
                        rows = slice(hh % 2 * HD, hh % 2 * HD + HD)
                        mm = nc.tensor.matmul(bank[b][:, j * P:(j + 1) * P], bT[rows, hh // 2, t * P:(t + 1) * P],
                                              AR[rows, hh // 2, t, 0, :], start=True, stop=True)
                    mm.then_inc(ba_ready, 1)
                pe.wait_ge(kd_ready, 1)
                srcs = [lambda k, t: AR[:, k, t, 0, :], lambda k, t: bT[:, k, t * P:(t + 1) * P],
                        lambda k, t: kdT[:, k, t * P:(t + 1) * P]]
                for i in range(12):
                    what, t, d = i // 4, i // 2 % 2, i % 2
                    if i >= 3:
                        pe.wait_ge(tok_out, i - 2)
                    for j in range(4):
                        mm = nc.tensor.transpose(bank[5 + i % 3][:, j * P:(j + 1) * P], srcs[what](4 * d + j, t), ident[:])
                    mm.then_inc(tok_turned, 1)

                def pairs_of(t):
                    for hh in range(RH):
                        rows = slice(hh % 2 * HD, hh % 2 * HD + HD)
                        n = t * RH + hh
                        b = bank[(0, 4)[hh % 2] + hh // 2 % 2]
                        if n >= 4:
                            pe.wait_ge(pairs_raw, n - 3)
                        ts = slice(t * P, (t + 1) * P)
                        nc.tensor.matmul(b[:, 0:P], bT[rows, hh // 2, ts], AR[rows, hh // 2, t, 1, :],
                                         start=True, stop=True)
                        nc.tensor.matmul(b[:, P:3 * P], kdT[rows, hh // 2, ts],
                                         AR[rows, hh // 2, t].rearrange("p a c -> p (a c)"),
                                         start=True, stop=True).then_inc(pairs_mm, 1)

                hs = lambda hh: slice(hh * HD, (hh + 1) * HD)

                def by_head(sta, mov, banks, sem_out):
                    for hh in range(RH):
                        mm = nc.tensor.matmul(banks[hh // 8][:, hh % 8 * HD:(hh % 8 + 1) * HD], sta(hh), mov(hh),
                                              start=True, stop=True)
                        if hh % 8 == 7:
                            mm.then_inc(sem_out, 1)

                pe.wait_ge(ba_out, 8)
                pe.wait_ge(tok_out, 12)
                def state_update(c, what, values, out_bank):
                    t, cc = divmod(c, 4)
                    rows = slice(cc * CH, (cc + 1) * CH)
                    for hh in range(RH):
                        e, j = hh % 2, hh // 2
                        mm = nc.tensor.matmul(out_bank[e * HD:(e + 1) * HD, j * HD:(j + 1) * HD],
                                              tok[rows, what, t, hs(hh)], values[rows, t, hs(hh)],
                                              start=j == 0, stop=j == KD - 1, skip_group_check=True,
                                              tile_position=(cc * CH, e * HD))
                    return mm

                for t in range(TT):
                    pairs_of(t)
                pe.wait_ge(pairs_raw, TT * RH)
                state_update(0, 2, v_tok, bank[3]).then_inc(kv_mm, 1)
                for t, b0 in enumerate((6, 2)):
                    pe.wait_ge(pairs_out, RH // 4 * (t + 1))
                    if t:
                        pe.wait_ge(kv_out, 1)
                    by_head(lambda hh: pairs[t][:, hh, 1, :], lambda hh: v_tok[:, t, hs(hh)], bank[b0:b0 + 2], x1_ready)
                pe.wait_ge(inv_back, 8 * 16)
                pe.wait_ge(x1_out, 4)
                for t, (b0, b1) in enumerate(((6, 2), (4, 0))):
                    by_head(lambda hh: inv[:, t, hh, :], lambda hh: U[:, t, hs(hh)], bank[b0:b0 + 2], u0_ready)
                    for hh in range(RH):
                        e, j = hh % 2, hh // 2
                        mm = nc.tensor.matmul(bank[b1 + j // 4][e * HD:(e + 1) * HD, j % 4 * P:(j % 4 + 1) * P],
                                              tok[:, 0, t, hs(hh)], inv[:, t, hh, :], start=True, stop=True)
                        if hh % 8 == 7:
                            mm.then_inc(wt_ready, 1)
                pe.wait_ge(u0_out, 4)
                pe.wait_ge(wt_out, 4)
                pe.wait_ge(ops_ready, 2)

                def outputs(t, heads):
                    for hh in heads:
                        out_ap = bank[6 + hh // 8][:, hh % 8 * HD:(hh % 8 + 1) * HD]
                        nc.tensor.matmul(out_ap, pairs[t][:, hh, 0, :], U[:, t, hs(hh)], start=True, stop=False)
                        mm = nc.tensor.matmul(out_ap, pairs[t][:, hh, 2, :], v_tok[:, t, hs(hh)], start=False, stop=True)
                        if hh % 8 == 7:
                            mm.then_inc(yg_ready, 1)

                for c in range(NC):
                    t, cc = divmod(c, 4)
                    rows, ts = slice(cc * CH, (cc + 1) * CH), slice(c * CH, (c + 1) * CH)
                    if c:
                        pe.wait_ge(s_ready, c)
                    for e in range(2):
                        hr = slice(e * HD, (e + 1) * HD)
                        for j in range(KD):
                            mm = nc.tensor.matmul(bank[e][rows, j * HD:(j + 1) * HD], WT[hr, j, ts], S[hr, j, :],
                                                  start=True, stop=True, tile_position=(e * HD, cc * CH))
                        mm.then_inc(u_mm, 1)
                    if c == 4:
                        pe.wait_ge(ys_out, 2)
                    for e in range(2):
                        hr = slice(e * HD, (e + 1) * HD)
                        for j in range(KD):
                            mm = nc.tensor.matmul(bank[4 + e][rows, j * HD:(j + 1) * HD],
                                                  AR[hr, j, t, 1, cc * CH:(cc + 1) * CH], S[hr, j, :],
                                                  start=True, stop=True, tile_position=(e * HD, cc * CH))
                    mm.then_inc(ys_ready, 1)
                    pe.wait_ge(u_ready, 2 * c + 2)
                    if c < NC - 1:
                        state_update(c, 1, U, bank[2]).then_inc(s_mm, 1)
                    if c < NC - 2:
                        pe.wait_ge(kv_out, c + 1)
                        state_update(c + 1, 2, v_tok, bank[3]).then_inc(kv_mm, 1)
                    if c in (4, 5):
                        outputs(0, range(8 * (c - 4), 8 * (c - 3)))
                pe.wait_ge(y_sum, 2)
                outputs(1, range(RH))
                for i in range(4):
                    t, d = divmod(i, 2)
                    pe.wait_ge(m_ready[t], d + 1)
                    for k in range(4):
                        mm = nc.tensor.transpose(bank[i][:, k * P:(k + 1) * P],
                                                 y_tok[:, t, (4 * d + k) * P:(4 * d + k + 1) * P], ident[:])
                    mm.then_inc(m_turned, 1)
                pe.wait_ge(m_split, 4)
                for i in range(2):
                    n = RWKV_OUT0 + i
                    for half in range(TT):
                        if i:
                            pe.wait_ge(h_ready, 4 * q + half + 1)
                        gate_up(n, n % 2, half)

            pe.wait_ge(consts, 4)
            for v in range(ADA_FRONT):
                if v >= 2:
                    pe.wait_ge(mods_ready, v - 1)
                ada_total(v, TB[v % 2])
            ffn(0, 0)
            dsa(1)
            ffn(1, 2)
            ffn(2, 3)
            rwkv(4)
            ffn(3, 5)

        @block.scalar
        def _(act):
            def load_ada(v, layer, hv, first=False):
                if not first:
                    act.wait_ge(ada_step, v * KD - KD + 1)
                act.dma_start(ada_bias[0:1, :], a["ada_b"][layer:layer + 1, bass.ds(hv * HALF, HALF)]
                              ).then_inc(bias_in, 16)
                for i in range(4):
                    if not first:
                        act.wait_ge(ada_step, v * KD + 2 * i - 6)
                    act.dma_start(ada_raw[:, i], ada_w[layer, :, 2 * i:2 * i + 2, bass.ds(hv * HALF, HALF)]
                                  ).then_inc(ada_in[i], 16)

            def copy_mods(v, hv, spread):
                act.wait_ge(ada_sum, v + 1)
                nc.scalar.copy(mods[:, bass.ds(hv, 1), :].rearrange("p a n -> p (a n)"), spread[:]).then_inc(mods_ready, 1)

            def round_block(n, par, first=False, width=HALF, buf=raw, free=False):
                if not (first or free):
                    act.wait_ge(g_ready[1], n - 1)
                for i in range(2):
                    act.wait_ge(raw_in[i], 32 * n + 32)
                    nc.scalar.copy(gu_hi[:, par, 4 * i:4 * i + 4, 0:width],
                                   buf[:, i, 0:4 * width].rearrange("p (k c) -> p k c", k=4)).then_inc(hi_ready[i], 1)

            def round_down(ub, first):
                if not first:
                    act.wait_ge(d_done[1], ub)
                act.wait_ge(raw_in[2], 16 * ub + 16)
                nc.scalar.copy(dn_hi[:], raw[:, 2, :].rearrange("p (t d) -> p t d", t=2)
                               ).then_inc(hi_ready[2], 1)

            def silu(n, ub, half, first=False):
                act.wait_ge(g_ready[half], n + 1)
                if not first:
                    act.wait_ge(t_ready[half], ub)
                nc.scalar.activation(hid[:, half, :], G[half][:, 0:FB], ACT.Silu).then_inc(silu_done[half], 1)

            def round_hidden(ub, half, first=False):
                act.wait_ge(t_ready[half], ub + 1)
                if not first:
                    act.wait_ge(d_done[half], ub)
                nc.scalar.copy(hT_hi[:, half], TB[half][:, 0:2 * P].rearrange("p (t c) -> p t c", t=2)
                               ).then_inc(hT_hi_ready[half], 1)

            def squares_of_h(q):
                act.wait_ge(h_in, 16)
                for t in range(TT):
                    if q:
                        act.wait_ge(h_ready, 4 * q if t else 4 * q - (1 if q in (2, 5) else 2))
                    if t:
                        act.wait_ge(square_sum, TT * q + t)
                    nc.scalar.activation(junk[:], h[:, t, :], ACT.Square,
                                         accum_out=stat[:, t:t + 1]).then_inc(square_sum, 1)

            def modulate(q, plain=False, squares_taken=False):
                if not squares_taken:
                    squares_of_h(q)
                act.wait_ge(rstd_var, q + 1)
                nc.scalar.activation(stat[:, 4:6], stat[:, 2:4], ACT.Sqrt).then_inc(root, 1)
                if q == 0:
                    round_block(0, 0, True)
                for i in range(4):
                    act.wait_ge(xn_turned, 4 * q + i + 1)
                    if plain:
                        nc.scalar.copy(uT[:, 4 * (i % 2):4 * (i % 2) + 4, (i // 2) * P:(i // 2 + 1) * P],
                                       bank[4 + i][:].rearrange("p (k c) -> p k c", k=4)).then_inc(uT_ready, 1)
                        continue
                    nc.scalar.copy(xT_hi[:, 4 * (i % 2):4 * (i % 2) + 4, (i // 2) * P:(i // 2 + 1) * P],
                                   bank[4 + i][:].rearrange("p (k c) -> p k c", k=4)).then_inc(xT_hi_ready, 1)

            def dsa(q):
                def round_in(i):
                    n = DSA_BLOCK0 + i
                    round_block(n, n % 2, width=DSA_IN[i][1] if i < len(DSA_IN) else HALF)

                load_ada(15, 0, 15)
                modulate(q)
                round_in(1)
                for i, (_, width, dst) in enumerate(DSA_IN):
                    for half in range(TT):
                        act.wait_ge(g_ready[half], DSA_BLOCK0 + i + 1)
                        nc.scalar.copy(dst(half), G[half][:, 0:width]).then_inc(z_out[half], 1)
                    round_in(i + 2)
                    if i in (1, 2, 3):
                        copy_mods(14 + i, 14 + i, TB[i % 2])
                    if i in (0, 1):
                        load_ada(16 + i, 0, 16 + i)
                    if i:
                        roots = {1: (0, 2), 2: (16, 16 + 2 * QH), 3: (4, 4 + 2 * KVH)}.get(i)
                        if roots:
                            r = dstat[:, roots[0]:roots[1]]
                            act.wait_ge(mean_ready, i)
                            nc.scalar.activation(r, r, ACT.Sqrt).then_inc(mean_root, 1)

                act.wait_ge(gains_in, 6 * 16)
                for g, (b, what, t, first) in enumerate(GROUPS):
                    act.wait_ge(group_turned, g + 1)
                    gain = {"q": 0, "k": 1, "ik": 2, "iq": None}[what]
                    src = bank[b][:].rearrange("p (j c) -> p j c", j=4)
                    if what == "ik":
                        dst, src = ikT[:], bank[b][:, 0:SEQ]
                    elif what == "q":
                        dst = qT[:, first:first + 4, t * P:(t + 1) * P]
                    else:
                        dst = (kT if what == "k" else iqT)[:, :, t * P:(t + 1) * P]
                    if gain is None:
                        nc.scalar.copy(dst, src).then_inc(group_out, 1)
                    else:
                        nc.scalar.activation(dst, src, ACT.Copy, scale=head_gain[:, gain:gain + 1]).then_inc(group_out, 1)
                for i, (b, _, _) in enumerate(SCORES):
                    act.wait_ge(scores_ready, i + 1)
                    act.wait_ge(k_normed, TT)
                    if i >= 2:
                        act.wait_ge(relu_used, i - 1)
                    nc.scalar.activation(relu[:, i % 2, :], bank[b][:], ACT.Relu).then_inc(relu_ready, 1)
                for i in range(2 * QH + 1):
                    if i < 2 * QH:
                        t = i % 2
                        act.wait_ge(max_ready, i + 1)
                        nc.scalar.activation(probs[:, i % 4, 0:(t + 1) * P], probs[:, i % 4, 0:(t + 1) * P], ACT.Exp,
                                             bias=dstat[:, 8 + i % 4:9 + i % 4],
                                             accum_out=dstat[:, 12 + i % 4:13 + i % 4]).then_inc(exp_ready, 1)
                    if i >= 4 and i % 2 == 0:
                        turned_probs(i // 2 - 2)
                for hh in range(QH - 1, QH):
                    turned_probs(hh)
                act.wait_ge(oT_out, QH // 2)
                for i in range(2):
                    ks = slice(4 * i, 4 * i + 4)
                    nc.scalar.copy(xT_hi[:, ks, :], oT[i]).then_inc(oT_hi_ready, 1)

            def turned_probs(hh):
                act.wait_ge(probs_turned, 2 * hh + 2)
                if hh >= 2:
                    act.wait_ge(o_ready, hh - 1)
                nc.scalar.copy(probsT[:, hh % 2, :], bank[4 + hh % 2][:, 0:3 * P]).then_inc(probsT_ready, 1)

            def rwkv(q):
                def r_in(n):
                    round_block(n, n % 2)

                modulate(q, plain=True)
                for i, (dst, src, fn) in enumerate((
                        (hid_wa[0:WA, :], bank[0][0:WA, 0:SEQ], ACT.Tanh),
                        (hid_wa[P - WA:P, :], bank[1][P - WA:P, 0:SEQ], ACT.Copy),
                        (hid_g[:, 0, :], bank[2][:, 0:SEQ], ACT.Sigmoid),
                        (hid_g[0:GL - P, 1, :], bank[3][0:GL - P, 0:SEQ], ACT.Sigmoid))):
                    act.wait_ge(lora_ready, i + 1)
                    nc.scalar.activation(dst, src, fn).then_inc(wa_hid_ready, 1)
                act.wait_ge(rwkv_in, 11 * 16)
                for m in range(KD):
                    act.wait_ge(wa_ready, m // 2 * 2 + 2)
                    for e, dst in ((0, sigT), (1, aT)):
                        nc.scalar.activation(dst[:, m, :], bank[4 * e + m // 2][:, m % 2 * SEQ:(m % 2 + 1) * SEQ],
                                             ACT.Sigmoid, bias=cols[:, e, m:m + 1]).then_inc(wa_out, 1)
                r_in(V_BLOCK + 1)

                def round_mix(i):
                    act.wait_ge(mix_ready, 4 + i)
                    if i:
                        act.wait_ge(g_ready[1], V_BLOCK + 2 * i)
                    else:
                        act.wait_ge(lora_ready, 4)
                    for half in range(2):
                        ks = slice(4 * half, 4 * half + 4)
                        nc.scalar.copy(xT_hi[:, ks, :], mix[2][:, ks, :]).then_inc(mix_hi_ready, 1)

                round_mix(0)
                for t in range(TT):
                    for d in range(2):
                        act.wait_ge(g_ready_rwkv, 2 * t + d + 1)
                        nc.scalar.copy(g_tok[:, t, d * HALF:(d + 1) * HALF], acc[t][d][:]).then_inc(g_out, 1)
                for i in range(2):
                    for half in range(TT):
                        act.wait_ge(g_ready[half], V_BLOCK + i + 1)
                        nc.scalar.copy(v_tok[:, half, i * HALF:(i + 1) * HALF], G[half][:]).then_inc(v_out, 1)
                    r_in(R_BLOCK + i)
                for i in range(4):
                    if i % 2 == 0:
                        round_mix(1 + i // 2)
                    if i == 2:
                        act.wait_ge(cum_ready, 1)
                        act.wait_ge(mix_split, 3)
                        nc.scalar.activation(decay_in[:], cum[:], ACT.Exp, scale=-DECAY).then_inc(decay_out, 1)
                        act.wait_ge(cum_ready, 2)
                        nc.scalar.activation(decay_before[:], decay_before[:], ACT.Exp, scale=-DECAY
                                             ).then_inc(decay_out, 1)
                        act.wait_ge(decay_out, 2)
                        nc.scalar.activation(cum[:], cum[:], ACT.Exp, scale=DECAY).then_inc(decay_out, 1)
                    for half in range(2):
                        act.wait_ge(g_ready[half], R_BLOCK + i + 1)
                        k0 = 4 * (i % 2) + 2 * half
                        src = G[half][:].rearrange("p (k c) -> p k c", k=2)
                        ins = nc.scalar.copy((rT if i < 2 else kTc)[:, k0:k0 + 2, :], src)
                        if i >= 2:
                            for k in range(2):
                                scale = cols[:, 2, k0 + k:k0 + k + 1]
                                nc.scalar.activation(kk[:, k0 + k, :], src[:, k, :], ACT.Copy, scale=scale)
                                ins = nc.scalar.activation(norm[:, k0 + k, :], src[:, k, :], ACT.Square, scale=scale)
                        ins.then_inc(rc_out, 1)
                        if i == 3:
                            for j in range(2 * half, 2 * half + 2):
                                act.wait_ge(kk_sum, j + 1)
                                nc.scalar.activation(norm[:, 2 * j:2 * j + 2, :],
                                                     bank[j][:].rearrange("p (k c) -> p k c", k=2), ACT.Sqrt
                                                     ).then_inc(kk_root, 1)
                    if i < 2:
                        r_in(K_BLOCK + i)
                act.wait_ge(bonus_ready, 1)
                nc.scalar.copy(rstat[:, 0:2 * RH], bank[4][:, 0:2 * RH]).then_inc(bonus_out, 1)
                for i in range(12):
                    what, t, d = i // 4, i // 2 % 2, i % 2
                    act.wait_ge(tok_turned, i + 1)
                    nc.scalar.copy(tok[:, what, t, d * HALF:(d + 1) * HALF], bank[5 + i % 3][:]).then_inc(tok_out, 1)
                for n in range(TT * RH):
                    t, hh = divmod(n, RH)
                    act.wait_ge(pairs_mm, n + 1)
                    nc.scalar.copy(pairs[t][:, hh], bank[(0, 4)[hh % 2] + hh // 2 % 2][:, 0:3 * P].rearrange(
                        "p (a c) -> p a c", a=3)).then_inc(pairs_raw, 1)

                def updates_out(chunks):
                    for c in chunks:
                        act.wait_ge(kv_mm, c + 1)
                        nc.scalar.copy(kv[:, c, :], bank[3][:]).then_inc(kv_out, 1)

                updates_out([0])
                for t, b0 in enumerate((6, 2)):
                    for d in range(2):
                        act.wait_ge(x1_ready, 2 * t + d + 1)
                        nc.scalar.copy(U[:, t, d * HALF:(d + 1) * HALF], bank[b0 + d][:]).then_inc(x1_out, 1)
                for t, (b0, b1) in enumerate(((6, 2), (4, 0))):
                    for d in range(2):
                        act.wait_ge(u0_ready, 2 * t + d + 1)
                        nc.scalar.copy(U0[:, t, d * HALF:(d + 1) * HALF], bank[b0 + d][:]).then_inc(u0_out, 1)
                    for d in range(2):
                        act.wait_ge(wt_ready, 2 * t + d + 1)
                        nc.scalar.copy(WT[:, 4 * d:4 * d + 4, t * P:(t + 1) * P],
                                       bank[b1 + d][:].rearrange("p (k c) -> p k c", k=4)).then_inc(wt_out, 1)
                for t in range(TT):
                    updates_out([(1, 2, 3), (4, 5, 6)][t])
                    act.wait_ge(ys_ready, 4 * t + 4)
                    for e in range(2):
                        nc.scalar.copy(y_tok[:, t, :].rearrange("p (j e c) -> p j e c", e=2, c=HD)[:, :, e, :],
                                       bank[4 + e][:].rearrange("p (j c) -> p j c", c=HD)).then_inc(ys_out, 1)
                round_block(RWKV_OUT0, 0, buf=out_raw, free=True)
                act.wait_ge(gn_var, 1)
                nc.scalar.activation(rstat[:, 64:64 + RH], rstat[:, 32:32 + RH], ACT.Sqrt).then_inc(gn_root, 1)
                act.wait_ge(yg_ready, 4)
                act.wait_ge(gn_var, 2)
                nc.scalar.activation(rstat[:, 64 + RH:64 + 2 * RH], rstat[:, 32 + RH:32 + 2 * RH], ACT.Sqrt
                                     ).then_inc(gn_root, 1)
                round_block(RWKV_OUT0 + 1, 1, free=True)
                for i in range(4):
                    act.wait_ge(m_turned, i + 1)
                    t, d = divmod(i, 2)
                    nc.scalar.copy(xT_hi[:, 4 * d:4 * d + 4, t * P:(t + 1) * P],
                                   bank[i][:].rearrange("p (k c) -> p k c", k=4)).then_inc(m_hi, 1)

            def ffn(f, q=None):
                if f in (1, 3):
                    round_block(FFN_BLOCK0[f], FFN_BLOCK0[f] % 2)
                if f:
                    modulate(q)
                n0 = FFN_BLOCK0[f]
                v0, nv = ADA_FFN[f]

                def step(b, odd, ada):
                    ub, n = f * NB + b, n0 + b
                    peeled = isinstance(b, int)
                    if not (peeled and b == 0):
                        silu(n - 1, ub - 1, 1, peeled and ub == 1)
                        round_hidden(ub - 1, 0, peeled and ub == 1)
                        round_down(ub - 1, peeled and ub == 1)
                    if ada:
                        load_ada(v0 + b, v0 // HV, v0 % HV + b)
                    if not (peeled and b == NB - 1):
                        round_block(n + 1, (n0 + odd + 1) % 2, peeled and n == 0)
                    silu(n, ub, 0, peeled and ub == 0)
                    if not (peeled and b == 0):
                        round_hidden(ub - 1, 1, peeled and ub == 1)
                        if nv and not (peeled and b > nv):
                            copy_mods(v0 + b - 1, v0 % HV + b - 1, TB[0])

                run_blocks(act, f, step)
                last = f * NB + NB - 1
                silu(n0 + NB - 1, last, 1)
                round_hidden(last, 0)
                round_down(last, False)
                round_hidden(last, 1)
                if f < 3:
                    round_block(n0 + NB, (n0 + NB) % 2, width=DSA_SMALL if f == 0 else HALF)
                if nv == NB:
                    copy_mods(v0 + NB - 1, v0 % HV + NB - 1, TB[0])

            act.wait_ge(c_in, 16)
            nc.scalar.activation(cact[:], ccol[:], ACT.Silu).then_inc(c_ready, 1)
            act.wait_ge(consts, 4)
            for v in range(ADA_FRONT):
                load_ada(v, 0, v, v == 0)
                if v:
                    copy_mods(v - 1, v - 1, TB[(v - 1) % 2])
            squares_of_h(0)
            copy_mods(ADA_FRONT - 1, ADA_FRONT - 1, TB[(ADA_FRONT - 1) % 2])
            modulate(0, squares_taken=True)
            ffn(0)
            dsa(1)
            ffn(1, 2)
            ffn(2, 3)
            rwkv(4)
            ffn(3, 5)

        @block.vector
        def _(dve):
            count = {"step": 0, "root": 0}

            def chain(ins):
                count["step"] += 1
                ins.then_inc(dve_step, 1)
                dve.wait_ge(dve_step, count["step"])

            def ada_products(v, first=False):
                dve.wait_ge(bias_in, 16 * v + 16)
                if not first:
                    dve.wait_ge(ada_sum, v)
                for k in range(KD):
                    if k % 2 == 0:
                        dve.wait_ge(ada_in[k // 2], 16 * v + 16)
                    if k:
                        dve.wait_ge(ada_step, v * KD + k)
                    nc.vector.scalar_tensor_tensor(out=ada_acc[:], in0=ada_raw[:, k // 2, k % 2, :],
                                                   scalar=cact[:, k:k + 1], in1=ada_acc[:] if k else ada_bias[:],
                                                   op0=ALU.mult, op1=ALU.add).then_inc(ada_step, 1)

            def rest_of_block(n, par, width=HALF, buf=raw):
                for i in range(2):
                    ks = slice(4 * i, 4 * i + 4)
                    dve.wait_ge(hi_ready[i], n + 1)
                    nc.vector.tensor_tensor(gu_lo[:, par, ks, 0:width],
                                            buf[:, i, 0:4 * width].rearrange("p (k c) -> p k c", k=4),
                                            gu_hi[:, par, ks, 0:width].bitcast(F32), ALU.subtract).then_inc(split[i], 1)

            def rest_of_down(ub):
                dve.wait_ge(hi_ready[2], ub + 1)
                nc.vector.tensor_tensor(dn_lo[:], raw[:, 2, :].rearrange("p (t d) -> p t d", t=2),
                                        dn_hi[:].bitcast(F32), ALU.subtract).then_inc(split[2], 1)

            def times_up(ub, half):
                dve.wait_ge(silu_done[half], ub + 1)
                nc.vector.tensor_tensor(hid[:, half, :], hid[:, half, :], G[half][:, FB:2 * FB], ALU.mult
                                        ).then_inc(hid_ready[half], 1)

            def rest_of_hidden(ub, half):
                dve.wait_ge(hT_hi_ready[half], ub + 1)
                nc.vector.tensor_tensor(hT_lo[:, half], TB[half][:, 0:2 * P].rearrange("p (t c) -> p t c", t=2),
                                        hT_hi[:, half].bitcast(F32), ALU.subtract).then_inc(hT_ready[half], 1)

            def modulate(q, shift, scale, mods_made, plain=False):
                dve.wait_ge(square_sum, TT * (q + 1))
                nc.vector.tensor_scalar(stat[:, 2:4], stat[:, 0:2], 1.0 / D, RMS_EPS, ALU.mult, ALU.add
                                        ).then_inc(rstd_var, 1)
                dve.wait_ge(root, q + 1)
                chain(nc.vector.reciprocal(stat[:, 6:8], stat[:, 4:6]))
                dve.wait_ge(mods_ready, mods_made)

                def rest_of_x(i):
                    t, d = divmod(i, 2)
                    dve.wait_ge(xT_hi_ready, 4 * (q if q < 4 else q - 1) + i + 1)
                    part = (slice(None), slice(4 * d, 4 * d + 4), slice(t * P, (t + 1) * P))
                    nc.vector.tensor_tensor(xT_lo[part], bank[4 + i][:].rearrange("p (k c) -> p k c", k=4),
                                            xT_hi[part].bitcast(F32), ALU.subtract).then_inc(xT_ready, 1)

                for i in range(4):
                    t, d = divmod(i, 2)
                    if i == 3 and not plain:
                        rest_of_x(0)
                    if i >= 2:
                        dve.wait_ge(xn_turned, 4 * q + i - 1)
                    chain(nc.vector.scalar_tensor_tensor(out=xn[:, d], in0=mods[:, 2 * scale + d], scalar=1.0,
                                                         in1=h[:, t, d * HALF:(d + 1) * HALF], op0=ALU.add, op1=ALU.mult))
                    nc.vector.scalar_tensor_tensor(out=xn[:, d], in0=xn[:, d], scalar=stat[:, 6 + t:7 + t],
                                                   in1=mods[:, 2 * shift + d], op0=ALU.mult, op1=ALU.add
                                                   ).then_inc(xn_ready, 1)
                if plain:
                    return
                rest_of_x(1)
                rest_of_x(2)
                rest_of_x(3)

            def residual(q, gate, factor, mods_made, last):
                dve.wait_ge(mods_ready, mods_made)
                for i in range(4):
                    t, d = divmod(i, 2)
                    dve.wait_ge(d_done[t], last + 1)
                    cols = slice(d * HALF, (d + 1) * HALF)
                    chain(nc.vector.scalar_tensor_tensor(out=xn[:, d], in0=acc[t][d][:], scalar=factor,
                                                         in1=mods[:, 2 * gate + d], op0=ALU.mult, op1=ALU.mult))
                    nc.vector.tensor_tensor(h[:, t, cols], h[:, t, cols], xn[:, d], ALU.add).then_inc(h_ready, 1)

            def rwkv(q):
                def rest_in(n):
                    rest_of_block(n, n % 2)

                dve.wait_ge(rwkv_in, 11 * 16)
                chain(nc.vector.memset(rk_heads[:], 0.0))
                for e in range(2):
                    rows = slice(e * HD, (e + 1) * HD)
                    nc.vector.tensor_copy(rk_heads[rows, :, e], cols[rows, 4, :]).then_inc(zeroed, 1)
                chain(nc.vector.tensor_scalar(cols[:, 5, :], cols[:, 3, :], -1.0, 1.0, ALU.mult, ALU.add))
                modulate(q, 3, 4, 36, plain=True)
                dve.wait_ge(uT_ready, 4)
                nc.vector.tensor_tensor(xxT[:, :, 1:SEQ], uT[:, :, 0:SEQ - 1], uT[:, :, 1:SEQ], ALU.subtract
                                        ).then_inc(zeroed, 1)
                nc.vector.tensor_scalar(xxT[:, :, 0:1], uT[:, :, 0:1], -1.0, None, ALU.mult).then_inc(zeroed, 1)
                dve.wait_ge(zeroed, 4)

                def mix_in(i, dst):
                    for k in range(KD):
                        ins = nc.vector.scalar_tensor_tensor(out=dst[:, k, :], in0=xxT[:, k, :], scalar=mu[:, i, k:k + 1],
                                                             in1=uT[:, k, :], op0=ALU.mult, op1=ALU.add)
                    ins.then_inc(mix_ready, 1)

                def rest_of_mix(i):
                    for half in range(2):
                        ks = slice(4 * half, 4 * half + 4)
                        dve.wait_ge(mix_hi_ready, 2 * i + half + 1)
                        ins = nc.vector.tensor_tensor(xT_lo[:, ks, :], mix[2][:, ks, :], xT_hi[:, ks, :].bitcast(F32),
                                                      ALU.subtract)
                    ins.then_inc(mix_split, 1)

                mix_in(3, mix[0])
                mix_in(4, mix[1])
                mix_in(5, mix[2])
                dve.wait_ge(lora_ready, 4)
                mix_in(2, mix[2])
                rest_of_mix(0)
                rest_in(V_BLOCK + 1)
                dve.wait_ge(mix_split, 1)
                mix_in(0, mix[2])
                dve.wait_ge(wa_out, 2 * KD)
                rest_in(R_BLOCK)
                rest_in(R_BLOCK + 1)
                rest_of_mix(1)
                dve.wait_ge(mix_split, 2)
                mix_in(1, mix[2])
                rest_in(K_BLOCK)
                rest_in(K_BLOCK + 1)
                rest_of_mix(2)
                dve.wait_ge(mix_split, 3)
                chain(nc.vector.memset(keep[:], 1.0))
                chain(nc.vector.memset(keep[:].rearrange("p (n c) -> p n c", c=CH)[:, :, 0:1], 0.0))
                nc.vector.tensor_tensor_scan(cum[:].rearrange("p k c -> p (k c)"), keep[:],
                                             sigT[:].rearrange("p k c -> p (k c)"), 0.0, ALU.mult, ALU.add
                                             ).then_inc(cum_ready, 1)
                dve.wait_ge(cum_ready, 1)
                nc.vector.tensor_tensor(decay_before[:], cum[:], sigT[:], ALU.subtract).then_inc(cum_ready, 1)
                dve.wait_ge(decay_out, 1)
                dve.wait_ge(g_ready[1], K_BLOCK + 1)
                parts = lambda x: x[:].rearrange("p k (t c) -> p k t c", t=TT)
                for t in range(TT):
                    nc.vector.tensor_tensor(AR[:, :, t, 1, :], parts(rT)[:, :, t, :], parts(decay_in)[:, :, t, :],
                                            ALU.mult)
                nc.vector.tensor_copy(chunk_decay[:], decay_in[:].rearrange("p k (n c) -> p k n c", c=CH)[:, :, :, CH - 1]
                                      ).then_inc(reads_ready, 1)
                dve.wait_ge(decay_out, 3)
                dve.wait_ge(gain_ready, 1)
                for half in range(2):
                    ks = slice(4 * half, 4 * half + 4)
                    dve.wait_ge(kk_root, 2 * half + 2)
                    chain(nc.vector.reciprocal(norm[:, ks, :], norm[:, ks, :]))
                    chain(nc.vector.scalar_tensor_tensor(out=kk[:, ks, :], in0=norm[:, ks, :], scalar=1e12,
                                                         in1=kk[:, ks, :], op0=ALU.min, op1=ALU.mult))
                    for t in range(TT):
                        nc.vector.scalar_tensor_tensor(out=AR[:, ks, t, 0, :], in0=parts(kk)[:, ks, t, :], scalar=-1.0,
                                                       in1=parts(decay_before)[:, ks, t, :], op0=ALU.mult, op1=ALU.mult)
                    chain(nc.vector.tensor_tensor(aT[:, ks, :], kk[:, ks, :], aT[:, ks, :], ALU.mult))
                dve.wait_ge(g_ready[1], RWKV_OUT0)
                nc.vector.tensor_tensor(bT[:], aT[:], cum[:], ALU.mult).then_inc(ops_ready, 1)
                dve.wait_ge(g_out, 4)
                nc.vector.memset(S[:], 0.0).then_inc(ops_ready, 1)
                dve.wait_ge(masks_made, 10)
                dve.wait_ge(kd_ready, 1)
                for i in range(8):
                    t, h0 = divmod(i, 4)
                    dve.wait_ge(ba_ready, i + 1)
                    dst = inv[:, t].rearrange("p (g j e) c -> p g j e c", g=2, e=2)[:, h0 // 2, :, h0 % 2, :]
                    nc.vector.tensor_tensor(dst, bank[2 * (h0 % 2)][:].rearrange("p (j c) -> p j c", j=4),
                                            masks[:, 0:1, :].broadcast_to([P, 4, P]), ALU.mult).then_inc(ba_out, 1)

                dve.wait_ge(ops_ready, 2)
                dve.wait_ge(bonus_out, 1)
                chain(nc.vector.memset(inv_out[:], 0.0))
                chain(nc.vector.memset(inv_out[:].rearrange("p s u -> p (s u)")[:, 0:CH * CH:CH + 1], 1.0))
                dve.wait_ge(inv_loaded, 16)
                for s_ in range(CH - 2, -1, -1):
                    n = CH - 1 - s_
                    tmp = inv_tmp[:, 0:n * n].rearrange("p (u s) -> p u s", u=n)
                    chain(nc.vector.tensor_tensor(tmp, inv_out[:, s_ + 1:CH, s_ + 1:CH].rearrange("p s u -> p u s"),
                                                  inv_in[:, s_:s_ + 1, s_ + 1:CH].broadcast_to([P, n, n]), ALU.mult))
                    ins = nc.vector.tensor_reduce(inv_out[:, s_, s_ + 1:CH], tmp, AX.X, ALU.add)
                    if s_:
                        chain(ins)
                    else:
                        ins.then_inc(inv_made, 1)
                def outputs_in(t):
                    for d in range(2):
                        ds = slice(d * HALF, (d + 1) * HALF)
                        dve.wait_ge(yg_ready, 2 * t + d + 1)
                        dve.wait_ge(ys_out, 2 * t + 2)
                        nc.vector.tensor_tensor(y_tok[:, t, ds], y_tok[:, t, ds], bank[6 + d][:], ALU.add
                                                ).then_inc(y_sum, 1)

                def one_over_deviation(t):
                    dve.wait_ge(gn_root, t + 1)
                    rstd = rstat[:, 64 + t * RH:64 + (t + 1) * RH]
                    nc.vector.reciprocal(rstd, rstd).then_inc(rstd_ready, 1)

                dve.wait_ge(u0_out, 4)
                for c in range(NC):
                    t, cc = divmod(c, 4)
                    rows = slice(cc * CH, (cc + 1) * CH)
                    heads = lambda x: x[rows, t, :].rearrange("p (j e c) -> p j e c", e=2, c=HD)
                    for e in range(2):
                        dve.wait_ge(u_mm, 2 * c + e + 1)
                        nc.vector.tensor_tensor(heads(U)[:, :, e, :], bank[e][rows, :].rearrange("p (j c) -> p j c", c=HD),
                                                heads(U0)[:, :, e, :], ALU.add).then_inc(u_ready, 1)
                    if c < NC - 1:
                        dve.wait_ge(ys_ready, c + 1)
                        dve.wait_ge(kv_out, c + 1)
                        chain(nc.vector.tensor_tensor(S[:], S[:], kv[:, c, :].rearrange("p (j c) -> p j c", c=HD),
                                                      ALU.add))
                        dve.wait_ge(s_mm, c + 1)
                        chain(nc.vector.tensor_tensor(S[:], S[:], bank[2][:].rearrange("p (j c) -> p j c", c=HD),
                                                      ALU.add))
                        nc.vector.tensor_tensor(S[:], S[:], chunk_decay[:, :, c:c + 1].broadcast_to([P, KD, HD]), ALU.mult
                                                ).then_inc(s_ready, 1)
                    if c == 6:
                        outputs_in(0)
                dve.wait_ge(y_sum, 2)
                group_norm(nc.vector, 0, chain).then_inc(gn_var, 1)
                one_over_deviation(0)
                rest_of_block(RWKV_OUT0, 0, buf=out_raw)
                outputs_in(1)
                dve.wait_ge(y_sum, 4)
                group_norm(nc.vector, 1, chain).then_inc(gn_var, 1)
                one_over_deviation(1)
                dve.wait_ge(rstd_ready, 2)
                dve.wait_ge(ln_in, 2 * 16)
                dve.wait_ge(bonus_out, 1)
                dve.wait_ge(g_out, 4)
                group_scale(nc.vector, 1, chain)
                for i in range(4):
                    t, d = divmod(i, 2)
                    dve.wait_ge(m_hi, i + 1)
                    part = (slice(None), slice(4 * d, 4 * d + 4), slice(t * P, (t + 1) * P))
                    nc.vector.tensor_tensor(xT_lo[part], bank[i][:].rearrange("p (k c) -> p k c", k=4),
                                            xT_hi[part].bitcast(F32), ALU.subtract).then_inc(m_split, 1)
                rest_in(RWKV_OUT0 + 1)
                for i in range(2):
                    if i:
                        rest_of_block(FFN_BLOCK0[3], FFN_BLOCK0[3] % 2)
                    for half in range(TT):
                        dve.wait_ge(g_ready[half], RWKV_OUT0 + i + 1)
                        cs = slice(i * HALF, (i + 1) * HALF)
                        chain(nc.vector.tensor_tensor(xn[:, half], G[half][:], mods[:, 2 * 5 + i], ALU.mult))
                        nc.vector.tensor_tensor(h[:, half, cs], h[:, half, cs], xn[:, half], ALU.add
                                                ).then_inc(h_ready, 1)

            def ffn(f, q):
                if f:
                    modulate(q, *((0, 1) if f % 2 == 0 else (6, 7)), (4, 18, 22, 36)[f])
                n0 = FFN_BLOCK0[f]
                v0, nv = ADA_FFN[f]

                def step(b, odd, ada):
                    ub, n = f * NB + b, n0 + b
                    peeled = isinstance(b, int)
                    if not (peeled and b == 0):
                        times_up(ub - 1, 1)
                        rest_of_hidden(ub - 1, 0)
                        rest_of_down(ub - 1)
                    if not (peeled and b == NB - 1):
                        rest_of_block(n + 1, (n0 + odd + 1) % 2)
                    times_up(ub, 0)
                    if not (peeled and b == 0):
                        rest_of_hidden(ub - 1, 1)
                    if ada:
                        ada_products(v0 + b)

                run_blocks(dve, f, step)
                last = f * NB + NB - 1
                times_up(last, 1)
                rest_of_hidden(last, 0)
                rest_of_down(last)
                rest_of_hidden(last, 1)
                if f < 3:
                    n = n0 + NB
                    rest_of_block(n, n % 2, DSA_SMALL if f == 0 else HALF)
                residual(q, 2 if f % 2 == 0 else 8, 0.5, (6, 18, 24, 36)[f], last)

            def head_norms(srcs, heads, s0):
                for t, src in enumerate(srcs):
                    sq = squares[:, 0:heads * HD]
                    chain(nc.vector.tensor_tensor(sq, src, src, ALU.mult))
                    r = dstat[:, s0 + t * heads:s0 + (t + 1) * heads]
                    chain(nc.vector.tensor_reduce(r, sq.rearrange("p (h c) -> p h c", h=heads), AX.X, ALU.add))
                r = dstat[:, s0:s0 + len(srcs) * heads]
                nc.vector.tensor_scalar(r, r, 1.0 / HD, RMS_EPS, ALU.mult, ALU.add).then_inc(mean_ready, 1)
                count["root"] += 1
                dve.wait_ge(mean_root, count["root"])
                chain(nc.vector.reciprocal(r, r))
                return [r[:, t * heads:(t + 1) * heads].unsqueeze(2).broadcast_to([P, heads, HD])
                        for t in range(len(srcs))]

            def dsa(q):
                def rest_in(i):
                    n = DSA_BLOCK0 + i
                    rest_of_block(n, n % 2, DSA_IN[i][1] if i < len(DSA_IN) else HALF)

                def heads_of(ap):
                    return ap.rearrange("p (h c) -> p h c", c=HD)

                modulate(q, 3, 4, 10)
                for i in range(3):
                    rest_in(i + 1)
                    ada_products(15 + i)
                for t in range(TT):
                    dve.wait_ge(z_out[t], 1)
                rs = head_norms([z_small[:, t, 0:HD] for t in range(TT)], 1, 0)
                for t in range(TT):
                    chain(nc.vector.tensor_tensor(ik_twice[:, t, 0:1, :], heads_of(z_small[:, t, 0:HD]), rs[t], ALU.mult))
                    chain(nc.vector.tensor_copy(ik_twice[:, t, 1:2, :], ik_twice[:, t, 0:1, :]))
                head_w = z_small[:, :, HD:HD + IH]
                nc.vector.tensor_scalar(head_w, head_w, IH ** -0.5 * HD ** -0.5, None, ALU.mult).then_inc(small_normed, 1)
                rest_in(4)
                for t in range(TT):
                    dve.wait_ge(z_out[t], 3)
                qs = [z[:, t, 0:QH * HD] for t in range(TT)]
                rs = head_norms(qs, QH, 16)
                for t in range(TT):
                    nc.vector.tensor_tensor(heads_of(qs[t]), heads_of(qs[t]), rs[t], ALU.mult).then_inc(q_normed, 1)
                rest_in(5)
                for t in range(TT):
                    dve.wait_ge(z_out[t], 4)
                ks = [z[:, t, 2 * HALF:2 * HALF + KVH * HD] for t in range(TT)]
                rs = head_norms(ks, KVH, 4)
                for t in range(TT):
                    if t:
                        dve.wait_ge(group_turned, 6)
                    chain(nc.vector.tensor_tensor(k_twice[:, :, 0, :], heads_of(ks[t]), rs[t], ALU.mult))
                    nc.vector.tensor_copy(k_twice[:, :, 1, :], k_twice[:, :, 0, :]).then_inc(k_normed, 1)
                dve.wait_ge(small_normed, 1)

                seen = [0, 0]
                for i, (_, t, heads) in enumerate(SCORES):
                    keys = (t + 1) * P
                    dve.wait_ge(relu_ready, i + 1)
                    for j, hh in enumerate(heads):
                        part = relu[:, i % 2, j * keys:(j + 1) * keys]
                        w = z_small[:, t, HD + hh:HD + hh + 1]
                        acc_t = score[:, t, 0:keys]
                        if seen[t] == 0:
                            ins = nc.vector.tensor_scalar(acc_t, part, w, None, ALU.mult)
                        else:
                            ins = nc.vector.scalar_tensor_tensor(out=acc_t, in0=part, scalar=w, in1=acc_t,
                                                                 op0=ALU.mult, op1=ALU.add)
                        seen[t] += 1
                        if j < len(heads) - 1:
                            chain(ins)
                    ins.then_inc(relu_used, 1)
                    dve.wait_ge(relu_used, i + 1)
                for t in range(TT):
                    keys = score[:, t, 0:(t + 1) * P]
                    dve.wait_ge(score_masked, t + 1)
                    for _ in range(TOPK // 8):
                        chain(nc.vector.max(top8[:], keys))
                        chain(nc.vector.match_replace(keys, top8[:], keys, TAKEN))
                    nc.vector.tensor_scalar(offset[:, t, 0:(t + 1) * P], keys, (NEG + TAKEN) / 2, HIDDEN, ALU.is_gt,
                                            ALU.mult).then_inc(offset_ready, 1)

                dve.wait_ge(offset_masked, TT)
                for i in range(2 * QH + 1):
                    if i < 2 * QH:
                        t = i % 2
                        keys = (t + 1) * P
                        dve.wait_ge(logits_ready, i + 1)
                        if i >= 4:
                            dve.wait_ge(probs_turned, i - 3)
                        p = probs[:, i % 4, 0:keys]
                        chain(nc.vector.tensor_tensor_reduce(p, bank[i % 4][:, 0:keys], offset[:, t, 0:keys],
                                                             HD ** -0.5, NEG, ALU.add, ALU.max,
                                                             dstat[:, 4 + i % 4:5 + i % 4]))
                        nc.vector.tensor_scalar(dstat[:, 8 + i % 4:9 + i % 4], dstat[:, 4 + i % 4:5 + i % 4], -1.0, None,
                                                ALU.mult).then_inc(max_ready, 1)
                    if i:
                        k = i - 1
                        dve.wait_ge(exp_ready, k + 1)
                        total = dstat[:, 12 + k % 4:13 + k % 4]
                        chain(nc.vector.reciprocal(total, total))
                        p = probs[:, k % 4, 0:(k % 2 + 1) * P]
                        nc.vector.tensor_scalar(p, p, total, None, ALU.mult).then_inc(probs_ready, 1)
                    if i >= 10 and i % 4 == 2:
                        heads_out((i - 10) // 4)
                for j in range(QH // 2 - 2, QH // 2):
                    heads_out(j)
                for i in range(2):
                    ks = slice(4 * i, 4 * i + 4)
                    dve.wait_ge(oT_hi_ready, i + 1)
                    nc.vector.tensor_tensor(xT_lo[:, ks, :], oT[i], xT_hi[:, ks, :].bitcast(F32), ALU.subtract
                                            ).then_inc(oT_ready, 1)
                rest_in(6)
                for i in range(2):
                    if i:
                        rest_of_block(FFN_BLOCK0[1], FFN_BLOCK0[1] % 2)
                    for half in range(TT):
                        dve.wait_ge(g_ready[half], DSA_OUT0 + i + 1)
                        cols = slice(i * HALF, (i + 1) * HALF)
                        chain(nc.vector.tensor_tensor(xn[:, half], G[half][:], mods[:, 2 * 5 + i], ALU.mult))
                        nc.vector.tensor_tensor(h[:, half, cols], h[:, half, cols], xn[:, half], ALU.add
                                                ).then_inc(h_ready, 1)

            def heads_out(j):
                dve.wait_ge(o_ready, 2 * j + 2)
                nc.vector.tensor_copy(oT[j // 4][:, j % 4, :], bank[6 + j % 2][:, 0:SEQ]).then_inc(oT_out, 1)

            dve.wait_ge(consts, 4)
            dve.wait_ge(c_ready, 1)
            for v in range(ADA_FRONT):
                ada_products(v, v == 0)
            modulate(0, 0, 1, 4)
            rest_of_block(0, 0)
            ffn(0, 0)
            dsa(1)
            ffn(1, 2)
            ffn(2, 3)
            rwkv(4)
            ffn(3, 5)


_INS = ['x', 'c', 'ada_w', 'ada_b', 'ffn_w_gu', 'ffn_w_down', 'dsa_w_in', 'dsa_q_norm', 'dsa_k_norm', 'dsa_ik_norm',
        'dsa_w_out', 'rwkv_mu', 'rwkv_w_rkv', 'rwkv_w0', 'rwkv_w1', 'rwkv_w2', 'rwkv_a0', 'rwkv_a1', 'rwkv_a2',
        'rwkv_g1', 'rwkv_g2', 'rwkv_k_k', 'rwkv_k_a', 'rwkv_r_k', 'rwkv_ln_w', 'rwkv_ln_b', 'rwkv_w_out']
_OUT = ((1, 256, 1024), 'float32')


def kernel(**inputs):
    import numpy as _np
    import concourse.bacc as _bacc
    from concourse import mybir as _mybir
    from concourse.bass_utils import run_bass_kernel_spmd as _run

    nc = _bacc.Bacc("TRN2", target_bir_lowering=False, num_devices=1)
    arrays, args = {}, {}
    for name in _INS:
        v = _np.ascontiguousarray(inputs[name])
        arrays[f"in_{name}_dram"] = v
        args[name] = nc.dram_tensor(f"in_{name}_dram", v.shape, _mybir.dt.from_np(v.dtype), kind="ExternalInput").ap()
    out = nc.dram_tensor("out_0_dram", _OUT[0], _mybir.dt.from_np(_np.dtype(_OUT[1])), kind="ExternalOutput").ap()
    trunk(nc, args, out)
    r = _run(nc, [arrays], core_ids=[0])
    return r.results[0]["out_0_dram"]
```
